# Optimizing a Trainium2 kernel written in Bass

```python
import math
import jax
import jax.numpy as jnp
from jax import lax
import numpy as np

D_MODEL = 1024
BATCH = 1
SEQ = 1024
DEPTH = 1

GRID_W = 64
CTX_LEN = 256
HY_WIDTH = 512
HY_ORDER = 2
HY_COLS = (HY_ORDER + 1) * HY_WIDTH
S5_WIDTH = 512
S5_GROUP = 16
S5_GROUPS = S5_WIDTH // S5_GROUP
S5_STATE = 64
MIX_WIDTH = HY_WIDTH + S5_WIDTH
IN_COLS = HY_COLS + S5_WIDTH
SHORT_CONV = 3
POS_EMB_DIM = 33
FILTER_WIDTH = 64
FILTER_OUT = HY_ORDER * 2 * HY_WIDTH
DECAY_FAST = 0.3
DECAY_SLOW = 1.5
DECAY_TARGET = 1e-2
N_EXPERTS = 16
EXPERT_FF = 2816
CAPACITY_FACTOR = 2
N_MOD = 6
NORM_EPS = 1e-6

kernel_name = "hybrid_hyena_s5_ec_dit_block"

def rmsnorm(x, g):
    xf = x.astype(jnp.float32)
    y = xf * lax.rsqrt(jnp.mean(xf * xf, axis=-1, keepdims=True) + NORM_EPS)
    return (y * g.astype(jnp.float32)).astype(x.dtype)

def adaln(cond, w, b):
    return jnp.split(jax.nn.silu(cond) @ w + b, N_MOD, axis=-1)

def modulate(h, shift, scale):
    return h * (1.0 + scale[:, None]) + shift[:, None]

def short_conv_rows(z, rows, w, b):
    bsz, length, ch = z.shape
    zr = z.reshape(bsz, rows, length // rows, ch)
    p = jnp.pad(zr, ((0, 0), (0, 0), (1, 1), (0, 0)))
    y = p[:, :, :-2] * w[0] + p[:, :, 1:-1] * w[1] + p[:, :, 2:] * w[2] + b
    return y.reshape(bsz, length, ch)

def hyena_filter_spectra(length, w1, b1, freq, w2, b2, w3, b3):
    f32 = jnp.float32
    w1, b1, freq, w2, b2, w3, b3 = [a.astype(f32) for a in (w1, b1, freq, w2, b2, w3, b3)]
    t = jnp.linspace(0.0, 1.0, length, dtype=f32)[:, None]
    bands = (POS_EMB_DIM - 1) // 2
    omega = 2.0 * math.pi * jnp.arange(length, dtype=f32)[:, None] / length
    f = jnp.linspace(1e-4, bands - 1, bands, dtype=f32)[None, :]
    feats = jnp.concatenate([t, jnp.cos(f * omega), -jnp.sin(f * omega)], axis=-1)
    h = jnp.sin(freq[0] * (feats @ w1 + b1))
    h = jnp.sin(freq[1] * (h @ w2 + b2))
    h = (h @ w3 + b3).reshape(length, HY_ORDER, 2, HY_WIDTH)
    deltas = jnp.abs(jnp.linspace(math.log(DECAY_TARGET) / DECAY_FAST,
                                  math.log(DECAY_TARGET) / DECAY_SLOW, HY_WIDTH, dtype=f32))
    h = h * jnp.exp(-t * deltas)[:, None, None, :]
    fwd, bwd = h[:, :, 0], h[:, :, 1]
    k = jnp.concatenate([fwd, jnp.zeros((1,) + fwd.shape[1:], f32), bwd[:0:-1]], axis=0)
    k = k / jnp.sum(jnp.abs(k), axis=0, keepdims=True)
    return jnp.fft.rfft(k, axis=0)

def long_conv(u, kf, bias):
    length = u.shape[1]
    uf = jnp.fft.rfft(u, n=2 * length, axis=1)
    y = jnp.fft.irfft(uf * kf[None], n=2 * length, axis=1)[:, :length]
    return y + u * bias.astype(jnp.float32)

def hyena_branch(z, rows, conv_w, conv_b, filt, hy_bias):
    length = z.shape[1]
    z = short_conv_rows(z, rows, conv_w, conv_b).astype(jnp.float32)
    v, x1, x2 = jnp.split(z, 3, axis=-1)
    kf = hyena_filter_spectra(length, *filt)
    y = x1 * long_conv(v, kf[:, 0], hy_bias[0])
    return x2 * long_conv(y, kf[:, 1], hy_bias[1])

def _diag_binop(e1, e2):
    a1, b1 = e1
    a2, b2 = e2
    return a1 * a2, a2 * b1 + b2

def s5_discretize(lam_re, lam_im, log_step, b_re, b_im):
    f32 = jnp.float32
    lam = lax.complex(lam_re.astype(f32), lam_im.astype(f32))
    lam_bar = jnp.exp(lam * jnp.exp(log_step.astype(f32))[:, None])
    b_bar = ((lam_bar - 1.0) / lam)[..., None] * lax.complex(b_re.astype(f32), b_im.astype(f32))
    return lam_bar, b_bar

def s5_scan(u_tm, lam_bar, b_bar, init, reverse):
    bu = jnp.einsum('lbgh,gph->lbgp', u_tm.astype(jnp.complex64), b_bar)
    edge = bu.shape[0] - 1 if reverse else 0
    bu = bu.at[edge].add(lam_bar * init)
    a = jnp.broadcast_to(lam_bar[None, None], (bu.shape[0], 1) + lam_bar.shape)
    _, states = lax.associative_scan(_diag_binop, (a, bu), reverse=reverse, axis=0)
    return states

def s5_states(u, lam_re, lam_im, log_step, b_re, b_im, init_f, init_b):
    bsz, length, _ = u.shape
    u_tm = jnp.transpose(u.reshape(bsz, length, S5_GROUPS, S5_GROUP), (1, 0, 2, 3))
    lam_f, bb_f = s5_discretize(lam_re[0], lam_im[0], log_step[0], b_re[0], b_im[0])
    lam_b, bb_b = s5_discretize(lam_re[1], lam_im[1], log_step[1], b_re[1], b_im[1])
    st_f = s5_scan(u_tm, lam_f, bb_f, init_f, False)
    st_b = s5_scan(u_tm, lam_b, bb_b, init_b, True)
    return st_f, st_b

def s5_readout(u, st_f, st_b, c_re, c_im, d, glu_w, glu_b):
    f32 = jnp.float32
    bsz, length, _ = u.shape
    c_f = lax.complex(c_re[0].astype(f32), c_im[0].astype(f32))
    c_b = lax.complex(c_re[1].astype(f32), c_im[1].astype(f32))
    y = jnp.real(jnp.einsum('lbgp,ghp->blgh', st_f, c_f) + jnp.einsum('lbgp,ghp->blgh', st_b, c_b))
    y = y.reshape(bsz, length, S5_WIDTH) + d.astype(f32) * u
    y = jax.nn.gelu(y)
    return y * jax.nn.sigmoid(y @ glu_w.astype(f32) + glu_b.astype(f32))

def expert_choice_ffn(h, router_w, w_gate, w_up, w_down):
    n, dm = h.shape[1], h.shape[2]
    cap = CAPACITY_FACTOR * n // N_EXPERTS
    aff = jax.nn.softmax(jnp.einsum('bnd,de->bne', h, router_w).astype(jnp.float32), axis=-1)
    gates, idx = lax.top_k(jnp.swapaxes(aff, 1, 2), cap)
    xg = jax.vmap(lambda hb, ib: hb[ib])(h, idx)

    def expert(args):
        xe, wg, wu, wd = args
        return (jax.nn.silu(xe @ wg) * (xe @ wu)) @ wd

    ye = lax.map(expert, (jnp.swapaxes(xg, 0, 1), w_gate, w_up, w_down))
    ye = jnp.swapaxes(ye, 0, 1) * gates[..., None].astype(h.dtype)
    return jax.vmap(lambda ib, yb: jnp.zeros((n, dm), yb.dtype).at[ib.reshape(-1)].add(yb.reshape(-1, dm)))(idx, ye)

def setup_inputs(seed: int = 0) -> dict:
    key = jax.random.key(seed)
    ks = iter(jax.random.split(key, 40))
    f32 = jnp.float32

    def nrm(shape, scale):
        return scale * jax.random.normal(next(ks), shape, f32)

    D, L = D_MODEL, DEPTH
    G, P, H = S5_GROUPS, S5_STATE, S5_GROUP
    return {
        "x": nrm((BATCH, SEQ, D), 1.0),
        "c": nrm((BATCH, D), 1.0),
        "ctx": nrm((BATCH, CTX_LEN, D), 1.0),
        "c_ctx": nrm((D,), 1.0),
        "mod_w": nrm((L, D, N_MOD * D), D ** -0.5),
        "mod_b": nrm((L, N_MOD * D), 0.01),
        "norm1_g": 1.0 + nrm((L, D), 0.02),
        "norm2_g": 1.0 + nrm((L, D), 0.02),
        "w_in": nrm((L, D, IN_COLS), D ** -0.5),
        "w_out": nrm((L, MIX_WIDTH, D), MIX_WIDTH ** -0.5),
        "conv_w": nrm((L, SHORT_CONV, HY_COLS), SHORT_CONV ** -0.5),
        "conv_b": nrm((L, HY_COLS), 0.01),
        "hy_w1": nrm((L, POS_EMB_DIM, FILTER_WIDTH), POS_EMB_DIM ** -0.5),
        "hy_b1": nrm((L, FILTER_WIDTH), 0.1),
        "hy_freq": 1.0 + nrm((L, 2, FILTER_WIDTH), 0.02),
        "hy_w2": nrm((L, FILTER_WIDTH, FILTER_WIDTH), FILTER_WIDTH ** -0.5),
        "hy_b2": nrm((L, FILTER_WIDTH), 0.1),
        "hy_w3": nrm((L, FILTER_WIDTH, FILTER_OUT), FILTER_WIDTH ** -0.5),
        "hy_b3": nrm((L, FILTER_OUT), 0.01),
        "hy_bias": nrm((L, HY_ORDER, HY_WIDTH), 1.0),
        "s5_lam_re": -0.5 + nrm((L, 2, G, P), 0.01),
        "s5_lam_im": math.pi * jnp.arange(P, dtype=f32) + nrm((L, 2, G, P), 0.01),
        "s5_log_step": jax.random.uniform(next(ks), (L, 2, G), f32, math.log(1e-3), math.log(1e-1)),
        "s5_b_re": nrm((L, 2, G, P, H), (2.0 * H) ** -0.5),
        "s5_b_im": nrm((L, 2, G, P, H), (2.0 * H) ** -0.5),
        "s5_c_re": nrm((L, 2, G, H, P), (2.0 * P) ** -0.5),
        "s5_c_im": nrm((L, 2, G, H, P), (2.0 * P) ** -0.5),
        "s5_d": nrm((L, S5_WIDTH), 1.0),
        "s5_glu_w": nrm((L, S5_WIDTH, S5_WIDTH), S5_WIDTH ** -0.5),
        "s5_glu_b": nrm((L, S5_WIDTH), 0.01),
        "router_w": nrm((L, D, N_EXPERTS), D ** -0.5),
        "ex_w_gate": nrm((L, N_EXPERTS, D, EXPERT_FF), D ** -0.5),
        "ex_w_up": nrm((L, N_EXPERTS, D, EXPERT_FF), D ** -0.5),
        "ex_w_down": nrm((L, N_EXPERTS, EXPERT_FF, D), EXPERT_FF ** -0.5),
        "final_g": 1.0 + nrm((D,), 0.02),
    }

def reference(x, c, ctx, c_ctx, mod_w, mod_b, norm1_g, norm2_g, w_in, w_out, conv_w, conv_b,
              hy_w1, hy_b1, hy_freq, hy_w2, hy_b2, hy_w3, hy_b3, hy_bias,
              s5_lam_re, s5_lam_im, s5_log_step, s5_b_re, s5_b_im, s5_c_re, s5_c_im, s5_d,
              s5_glu_w, s5_glu_b, router_w, ex_w_gate, ex_w_up, ex_w_down, final_g):
    rows = x.shape[1] // GRID_W
    bsz = x.shape[0]
    for l in range(DEPTH):
        last = l == DEPTH - 1
        sh1, sc1, g1, sh2, sc2, g2 = adaln(c, mod_w[l], mod_b[l])
        csh1, csc1, cg1, csh2, csc2, cg2 = adaln(c_ctx[None], mod_w[l], mod_b[l])
        filt = (hy_w1[l], hy_b1[l], hy_freq[l], hy_w2[l], hy_b2[l], hy_w3[l], hy_b3[l])
        s5_par = (s5_lam_re[l], s5_lam_im[l], s5_log_step[l], s5_b_re[l], s5_b_im[l])
        s5_out = (s5_c_re[l], s5_c_im[l], s5_d[l], s5_glu_w[l], s5_glu_b[l])

        hc = modulate(rmsnorm(ctx, norm1_g[l]), csh1, csc1)
        u_c = (hc @ w_in[l][:, HY_COLS:]).astype(jnp.float32)
        zero = jnp.zeros((bsz, S5_GROUPS, S5_STATE), jnp.complex64)
        stc_f, stc_b = s5_states(u_c, *s5_par, zero, zero)
        init_f, init_b = stc_f[-1], stc_b[0]
        if not last:
            yc = jnp.concatenate([hyena_branch(hc @ w_in[l][:, :HY_COLS], 1, conv_w[l], conv_b[l], filt, hy_bias[l]),
                                  s5_readout(u_c, stc_f, stc_b, *s5_out)], axis=-1)
            ctx = ctx + cg1[:, None] * (yc.astype(ctx.dtype) @ w_out[l])
            hc2 = modulate(rmsnorm(ctx, norm2_g[l]), csh2, csc2)
            ctx = ctx + cg2[:, None] * expert_choice_ffn(hc2, router_w[l], ex_w_gate[l], ex_w_up[l], ex_w_down[l])

        h = modulate(rmsnorm(x, norm1_g[l]), sh1, sc1)
        z = h @ w_in[l]
        u = z[..., HY_COLS:].astype(jnp.float32)
        st_f, st_b = s5_states(u, *s5_par, init_f, init_b)
        y = jnp.concatenate([hyena_branch(z[..., :HY_COLS], rows, conv_w[l], conv_b[l], filt, hy_bias[l]),
                             s5_readout(u, st_f, st_b, *s5_out)], axis=-1)
        x = x + g1[:, None] * (y.astype(x.dtype) @ w_out[l])
        h2 = modulate(rmsnorm(x, norm2_g[l]), sh2, sc2)
        x = x + g2[:, None] * expert_choice_ffn(h2, router_w[l], ex_w_gate[l], ex_w_up[l], ex_w_down[l])
    return rmsnorm(x, final_g)


_drawn_inputs = setup_inputs


def setup_inputs(seed=0):
    import zlib

    import numpy as np

    out = dict(_drawn_inputs(seed))
    spreads = {}
    factors = {'ctx': 7.234,
     'c_ctx': 5.882,
     'norm2_g': 2.953,
     'conv_b': 3.532,
     'hy_freq': 7.3,
     'hy_b3': 4.465,
     's5_lam_re': 8.0,
     's5_log_step': 2.907,
     's5_b_re': 2.98,
     's5_b_im': 2.987,
     's5_c_re': 2.834,
     's5_glu_b': 8.0,
     'final_g': 2.841}
    for name, (base, spread) in spreads.items():
        noise = np.random.default_rng([zlib.crc32(name.encode()), seed]).standard_normal(out[name].shape)
        drawn = base * np.exp(spread * noise) if base else spread * noise
        out[name] = jnp.asarray(drawn.astype(out[name].dtype))
    for name, factor in factors.items():
        out[name] = (out[name] * factor).astype(out[name].dtype)
    return out
```

```python
import math
from contextlib import ExitStack

import concourse.bass as bass
import numpy as np
from concourse import mybir

F32 = mybir.dt.float32
I32 = mybir.dt.int32
U32 = mybir.dt.uint32
ALU = mybir.AluOpType
ACT = mybir.ActivationFunctionType
AX = mybir.AxisListType

P = 128
D = 1024
SEQ = 1024
CTX = 256
TOK = CTX + SEQ
KD = D // P
GRID = 64
HY = 512
HQ = HY // P
S5W = 512
NG, NP, NH = 32, 64, 16
PAIRS = NG // 2
T = 8
CH = TOK // T
CCH = CTX // T
XCH = SEQ // T
EPS = 1e-6
NE, FF, CAP = 16, 2816, 128
HALF = SEQ // 2
FEATS, FW = 33, 64
ROUND = 12582912.0
TURN = 6.2831845
INV_TURN = 1.0 / (2.0 * math.pi)
NEXP = 2 * (T + 1)

ROWS = {"c": (0, 8), "c_ctx": (8, 8), "norm1": (16, 8), "conv": (24, 36), "conv_b": (60, 12),
        "d": (72, 4), "glu_b": (76, 4)}
NROWS = 80


def shape_constants():
    f = np.arange(HALF, dtype=np.float64)
    tp = np.arange(HALF, dtype=np.float64)
    out = {}

    def tiles(m):
        return m.reshape(4, P, -1).transpose(1, 0, 2)

    def blocks(mats):
        a = np.stack([tiles(m) for m in mats], 1)
        return np.ascontiguousarray(a.reshape(P, 4, 4, 4, P).transpose(3, 0, 1, 2, 4)).astype(np.float32)

    def ang(shift):
        return [2 * np.pi * np.outer(2 * tp + par + shift, f + 0.5) / (2 * SEQ) for par in range(2)]

    even, odd = ang(0.0)
    out["dft_filter"] = blocks([np.cos(even), np.cos(odd), np.sin(even), np.sin(odd)])
    even, odd = ang(0.5)
    out["dft_signal"] = blocks([np.cos(even), np.cos(odd), np.sin(even), np.sin(odd)])
    inv = [fn(a).T / SEQ for a in (even, odd) for fn in (np.cos, np.sin)]
    out["dft_inverse"] = np.ascontiguousarray(np.stack([tiles(m) for m in inv])).astype(np.float32)

    t = np.concatenate([np.arange(0, SEQ, 2), np.arange(1, SEQ, 2)])
    tt = np.linspace(0.0, 1.0, SEQ, dtype=np.float32)[t].astype(np.float64)
    bands = (FEATS - 1) // 2
    omega = 2.0 * np.pi * t / SEQ
    fr = np.linspace(1e-4, bands - 1, bands)
    out["feats_t"] = np.concatenate([tt[None], np.cos(np.outer(fr, omega)), -np.sin(np.outer(fr, omega))]).astype(np.float32)
    deltas = np.abs(np.linspace(math.log(1e-2) / 0.3, math.log(1e-2) / 1.5, HY))
    out["decay"] = np.ascontiguousarray(np.exp(-np.outer(tt, deltas)).reshape(8, P, HY).transpose(1, 0, 2)).astype(np.float32)
    steps = np.concatenate([np.arange(T + 1), np.arange(T, -1, -1), np.arange(CH)])
    out["steps"] = np.tile(steps.astype(np.float32), (P, 1))
    out["identity"] = np.eye(P, dtype=np.float32)
    return out


class Links:

    def __init__(self, eng, sem):
        self.eng, self.sem, self.n = eng, sem, 0

    def __call__(self, ins):
        self.n += 1
        ins.then_inc(self.sem, 1)
        self.eng.wait_ge(self.sem, self.n)


def bcast(ap, shape):
    return ap.unsqueeze(len(shape) - 1).to_broadcast(shape)


class Core:

    def __init__(self, nc, ctx, ins, consts, out):
        self.nc, self.ctx, self.i, self.c, self.out = nc, ctx, ins, consts, out
        self.arena = ctx.enter_context(nc.sbuf_tensor("arena", [P, 52224], F32))
        self.ps = ctx.enter_context(nc.psum_tensor("psum", [P, 8, 512], F32))
        a = self.arena
        kb = 256

        def at(first, n, start=0):
            return a[:, (start + first) * kb:(start + first) * kb + n * kb]

        self.at = at
        self.greg = at(0, 32)
        self.x2t = at(32, 16).rearrange("p (q t) -> p q t", q=HQ)
        self.v = at(48, 16).rearrange("p (j c) -> p j c", j=8)
        self.x1 = at(64, 16).rearrange("p (j c) -> p j c", j=8)
        self.h_t = at(48, 40).rearrange("p (k t) -> p k t", k=KD)
        self.spec = at(88, 32).rearrange("p (a f c) -> p a f c", a=4, f=4)
        self.ring = at(120, 32).rearrange("p (s n) -> p s n", s=4)
        self.tmp = at(152, 24)
        self.bc = at(176, 20).rearrange("p (b n) -> p b n", b=5)
        small = at(196, 8)
        self.cols = small[:, 0:NROWS]
        self.mod_cols = small[:, 80:112].rearrange("p (j w) -> p j w", w=2)
        self.ident = small[:, 128:256]
        self.ones = small[:, 256:384]
        self.rstd = small[:, 384:400]
        self.inv_col = small[:, 400:404]
        self.scale1 = small[:, 404:420].rearrange("p (w k) -> p w k", w=2)
        self.gate_t = small[:, 420:436]
        self.idx_t = small[:, 436:452].bitcast(I32)
        self.idx_now = small[:, 452:453].bitcast(U32)
        self.silu_c = small[:, 460:476]
        self.inv_row = small[:, 512:1024]
        self.small = small
        self.extra = small[:, 1024:2048]
        self.G1, self.A2, self.SH2, self.G2, self.FG = range(5)
        self.z_u = nc.dram_tensor("scratch_u", (S5W, T, CH), F32).ap()
        self.z_y = nc.dram_tensor("scratch_y", (S5W, T, XCH), F32).ap()
        self.h2 = nc.dram_tensor("scratch_h2", (SEQ, D), F32).ap()
        self.moe = nc.dram_tensor("scratch_moe", (SEQ, D), F32).ap()

        self.stage_sems = []

    def sem(self, name):
        self.stage_sems.append(self.nc.alloc_semaphore(name=name))
        return self.stage_sems[-1]

    def end_stage(self):
        if self.stage_sems:
            self.nc.clear_and_free_semaphores(self.stage_sems)
            self.nc.all_engine_barrier()
        self.stage_sems = []


def modulation(k):
    nc, ps = k.nc, k.ps
    rows = k.tmp[0:NROWS, 0:P]
    mod_rows = k.tmp[0:2, 128:128 + 2 * D]
    bias = k.tmp[:, 2304:2304 + 2 * 512].rearrange("p (b n) -> p b n", b=2)
    wbuf = k.at(120, 32).rearrange("p (s k n) -> p s k n", s=2, k=KD)
    wmod = k.i["mod_w"].rearrange("l (k p) n -> p (l k) n", p=P)
    norm2 = k.tmp[:, 3400:3400 + D]
    loaded, ready, turned, silu, wgot = k.sem("m_rows"), k.sem("m_const"), k.sem("m_turned"), k.sem("m_silu"), [k.sem(f"m_w{s}") for s in range(2)]
    bgot = [k.sem(f"m_b{s}") for s in range(2)]
    mm, ev, tr, rows_in, own, zeroed = k.sem("m_mm"), k.sem("m_ev"), k.sem("m_tr"), k.sem("m_bc"), k.sem("m_own"), k.sem("m_zero")
    NCH = 6 * D // 512

    with nc.Block() as block:
        @block.sync
        def _(sp):
            def rows_of(name, ap):
                r, n = ROWS[name]
                sp.dma_start(rows[r:r + n, :], ap).then_inc(loaded, 16)
            rows_of("c", k.i["c"].rearrange("b (k p) -> (b k) p", p=P))
            rows_of("c_ctx", k.i["c_ctx"].rearrange("(k p) -> k p", p=P))
            rows_of("norm1", k.i["norm1_g"].rearrange("b (k p) -> (b k) p", p=P))
            rows_of("conv", k.i["conv_w"].rearrange("l w (k p) -> (l w k) p", p=P))
            rows_of("conv_b", k.i["conv_b"].rearrange("b (k p) -> (b k) p", p=P))
            rows_of("d", k.i["s5_d"].rearrange("b (k p) -> (b k) p", p=P))
            rows_of("glu_b", k.i["s5_glu_b"].rearrange("b (k p) -> (b k) p", p=P))
            sp.dma_start(k.ident, k.c["identity"]).then_inc(loaded, 16)
            for n in range(NCH):
                if n >= 2:
                    sp.wait_ge(mm, n - 1)
                    sp.wait_ge(ev, n - 1)
                sp.dma_start(wbuf[:, n % 2], wmod[:, :, n * 512:(n + 1) * 512]).then_inc(wgot[n % 2], 16)
                sp.dma_start(bias[:, n % 2, :], k.i["mod_b"][0:1, n * 512:(n + 1) * 512].to_broadcast([P, 512])).then_inc(bgot[n % 2], 16)

        @block.gpsimd
        def _(pool):
            nc.gpsimd.memset(k.ones, 1.0).then_inc(ready, 1)
            nc.gpsimd.memset(k.spec, 0.0).then_inc(ready, 1)
            pool.dma_start(norm2, k.i["norm2_g"].to_broadcast([P, D])).then_inc(rows_in, 16)
            pool.dma_start(k.bc[:, k.FG, :], k.i["final_g"].rearrange("(a n) -> a n", a=1).to_broadcast([P, D])).then_inc(rows_in, 16)
            pool.wait_ge(ready, 2)
            pool.dma_start(k.moe.rearrange("(p r) n -> p (r n)", p=P), k.spec.rearrange("p a f c -> p (a f c)")).then_inc(zeroed, 16)
            pool.wait_ge(zeroed, 16)

        @block.tensor
        def _(pe):
            pe.wait_ge(loaded, 128)
            nc.tensor.transpose(ps[:, 7, 0:NROWS], rows, k.ident[0:NROWS, 0:NROWS]).then_inc(turned, 1)
            pe.wait_ge(silu, 1)
            for n in range(NCH):
                pe.wait_ge(wgot[n % 2], 16 * (n // 2 + 1))
                if n >= 2:
                    pe.wait_ge(ev, n - 1)
                for kk in range(KD):
                    if n < 4:
                        lhs, o = k.silu_c[:, kk::KD], ps[0:2, n % 2, :]
                    else:
                        lhs, o = k.silu_c[:, kk:kk + 1].to_broadcast([P, P]), ps[:, n % 2, :]
                    last = nc.tensor.matmul(o, lhs, wbuf[:, n % 2, kk, :], start=kk == 0, stop=kk == KD - 1)
                last.then_inc(mm, 1)
                if n == 4:
                    pe.wait_ge(ev, 4)
                    for j in range(16):
                        last = nc.tensor.transpose(ps[:, 6, 2 * j:2 * j + 2], mod_rows[:, j * P:(j + 1) * P], k.ident[0:2, 0:2])
                    last.then_inc(tr, 1)

        @block.scalar
        def _(act):
            act.wait_ge(turned, 1)
            nc.scalar.activation(k.silu_c, ps[:, 7, 0:16], ACT.Silu).then_inc(silu, 1)

        @block.vector
        def _(dve):
            link = Links(dve, own)
            dve.wait_ge(turned, 1)
            dve.wait_ge(silu, 1)
            link(nc.vector.tensor_copy(k.cols, ps[:, 7, 0:NROWS]))
            for n in range(NCH):
                dve.wait_ge(mm, n + 1)
                dve.wait_ge(bgot[n % 2], 16 * (n // 2 + 1))
                p = slice(0, 2) if n < 4 else slice(0, P)
                if n < 4:
                    o = mod_rows[:, n * 512:(n + 1) * 512]
                else:
                    which, h = divmod(n - 4, 2)
                    o = k.bc[:, [k.G1, k.SH2, k.A2, k.G2][which], h * 512:(h + 1) * 512]
                nc.vector.tensor_tensor(o, ps[p, n % 2, :], bias[p, n % 2, :], ALU.add).then_inc(ev, 1)
            dve.wait_ge(ev, NCH)
            dve.wait_ge(tr, 1)
            link(nc.vector.tensor_copy(k.mod_cols, ps[:, 6, 0:32].rearrange("p (j w) -> p j w", w=2)))
            r = ROWS["norm1"][0]
            for w in range(2):
                nc.vector.scalar_tensor_tensor(k.scale1[:, w, :], k.mod_cols[:, 8:16, w], 1.0, k.cols[:, r:r + 8], ALU.add, ALU.mult)
            dve.wait_ge(rows_in, 32)
            link(nc.vector.scalar_tensor_tensor(k.bc[:, k.A2, :], k.bc[:, k.A2, :], 1.0, norm2, ALU.add, ALU.mult))


def projection(k):
    nc, ps = k.nc, k.ps
    NT = TOK // P
    xin = k.at(120, 12).rearrange("p (s n) -> p s n", s=3)
    xn = k.at(132, 8).rearrange("p (s n) -> p s n", s=2)
    sq = k.at(140, 4)
    got, ss, own_v, own_s, norm, tr, ev, tdone = k.sem("p_x"), k.sem("p_ss"), k.sem("p_dve"), k.sem("p_act"), k.sem("p_norm"), k.sem("p_tr"), k.sem("p_ev"), k.sem("p_sqrt")
    got3 = [k.sem(f"p_x{s}") for s in range(3)]

    with nc.Block() as block:
        @block.sync
        def _(sp):
            for n in range(NT):
                if n >= 3:
                    sp.wait_ge(norm, n - 2)
                src = k.i["ctx"][0, n * P:(n + 1) * P, :] if n < 2 else k.i["x"][0, (n - 2) * P:(n - 1) * P, :]
                sp.dma_start(xin[:, n % 3, :], src).then_inc(got3[n % 3], 16)

        @block.scalar
        def _(act):
            for n in range(NT):
                act.wait_ge(got3[n % 3], 16 * (n // 3 + 1))
                if n:
                    act.wait_ge(ss, n)
                nc.scalar.activation(sq, xin[:, n % 3, :], ACT.Square, accum_out=k.rstd[:, n:n + 1]).then_inc(ss, 1)
                act.wait_ge(own_v, 1 + 2 * n)
                nc.scalar.activation(k.rstd[:, n:n + 1], k.rstd[:, n:n + 1], ACT.Sqrt).then_inc(tdone, 1)

        def evacuate(dve, n):
            dve.wait_ge(tr, n + 1)
            w = 1 if n < 2 else 0
            for kk in range(KD):
                last = nc.vector.tensor_scalar(k.h_t[:, kk, n * P:(n + 1) * P], ps[:, 2 * (n % 2) + kk // 4, (kk % 4) * P:(kk % 4 + 1) * P],
                                               k.scale1[:, w, kk:kk + 1], k.mod_cols[:, kk, w:w + 1], ALU.mult, ALU.add)
            last.then_inc(ev, 1)

        @block.vector
        def _(dve):
            link = Links(dve, own_v)
            for n in range(NT):
                dve.wait_ge(ss, n + 1)
                r = k.rstd[:, n:n + 1]
                link(nc.vector.tensor_scalar(r, r, 1.0 / D, EPS, ALU.mult, ALU.add))
                dve.wait_ge(tdone, n + 1)
                link(nc.vector.reciprocal(r, r))
                if n >= 2:
                    dve.wait_ge(tr, n - 1)
                nc.vector.tensor_scalar(xn[:, n % 2, :], xin[:, n % 3, :], r, None, ALU.mult).then_inc(norm, 1)
                if n:
                    evacuate(dve, n - 1)
            evacuate(dve, NT - 1)

        @block.tensor
        def _(pe):
            for n in range(NT):
                pe.wait_ge(norm, n + 1)
                if n >= 2:
                    pe.wait_ge(ev, n - 1)
                for kk in range(KD):
                    last = nc.tensor.transpose(ps[:, 2 * (n % 2) + kk // 4, (kk % 4) * P:(kk % 4 + 1) * P], xn[:, n % 2, kk * P:(kk + 1) * P], k.ident)
                last.then_inc(tr, 1)

    z_t = k.greg.rearrange("p (q t) -> p q t", q=2 * HQ)
    wbuf = k.at(120, 32).rearrange("p (s k n) -> p s k n", s=4, k=KD)
    w_in = k.i["w_in"].rearrange("l (k p) n -> p (l k) n", p=P)
    ubuf = k.tmp[:, 0:2 * TOK].rearrange("p (s n) -> p s n", s=2)
    wgot = [k.sem(f"p_w{s}") for s in range(4)]
    mm, mid, conv, uout, own2 = k.sem("p_mm"), k.sem("p_mid"), k.sem("p_conv"), [k.sem(f"p_uout{s}") for s in range(2)], k.sem("p_own2")
    NCT = 16
    with nc.Block() as block:
        @block.sync
        def _(sp):
            for g in range(NCT // 2):
                if g >= 4:
                    sp.wait_ge(mm, 2 * g - 6)
                sp.dma_start(wbuf[:, g % 4], w_in[:, :, g * 256:(g + 1) * 256]).then_inc(wgot[g % 4], 16)
            for q in range(HQ):
                sp.wait_ge(conv, 12 + q + 1)
                sp.dma_start(k.z_u[q * P:(q + 1) * P].rearrange("p s k -> p (s k)"), ubuf[:, q % 2, :]).then_inc(uout[q % 2], 16)
            sp.wait_ge(uout[0], 32)
            sp.wait_ge(uout[1], 32)

        @block.tensor
        def _(pe):
            for c in range(NCT):
                if c % 2 == 0:
                    pe.wait_ge(wgot[(c // 2) % 4], 16 * (c // 8 + 1))
                if c >= 2:
                    pe.wait_ge(conv, c - 1)
                b0 = 4 * (c % 2)
                spans = [(CTX, 512), (CTX + 512, 512)] + ([(0, CTX)] if c >= 12 else [])
                for b, (t0, n) in enumerate(spans):
                    for kk in range(KD):
                        last = nc.tensor.matmul(ps[:, b0 + b, 0:n], wbuf[:, (c // 2) % 4, kk, (c % 2) * P:(c % 2 + 1) * P],
                                                k.h_t[:, kk, t0:t0 + n], start=kk == 0, stop=kk == KD - 1)
                last.then_inc(mm, 1)

        def out_of(c):
            if c < 8:
                return z_t[:, c, :]
            return k.x2t[:, c - 8, :]

        @block.scalar
        def _(act):
            for c in range(12):
                act.wait_ge(mm, c + 1)
                r0, rb = ROWS["conv"][0], ROWS["conv_b"][0]
                z = ps[:, 4 * (c % 2):4 * (c % 2) + 2, :].rearrange("p b n -> p (b n)")
                nc.scalar.activation(out_of(c), z, ACT.Identity, bias=k.cols[:, rb + c:rb + c + 1], scale=k.cols[:, r0 + 12 + c:r0 + 13 + c]).then_inc(mid, 1)

        @block.vector
        def _(dve):
            link = Links(dve, own2)
            for c in range(12):
                dve.wait_ge(mid, c + 1)
                z = ps[:, 4 * (c % 2):4 * (c % 2) + 2, :].rearrange("p b (r t) -> p (b r) t", t=GRID)
                o = out_of(c).rearrange("p (r t) -> p r t", t=GRID)
                r0 = ROWS["conv"][0]
                link(nc.vector.scalar_tensor_tensor(o[:, :, 1:GRID], z[:, :, 0:GRID - 1], k.cols[:, r0 + c:r0 + c + 1], o[:, :, 1:GRID], ALU.mult, ALU.add))
                nc.vector.scalar_tensor_tensor(o[:, :, 0:GRID - 1], z[:, :, 1:GRID], k.cols[:, r0 + 24 + c:r0 + 25 + c], o[:, :, 0:GRID - 1], ALU.mult, ALU.add).then_inc(conv, 1)
            for q in range(HQ):
                c = 12 + q
                dve.wait_ge(mm, c + 1)
                if q >= 2:
                    dve.wait_ge(uout[q % 2], 16)
                o = ubuf[:, q % 2, :].rearrange("p (s k) -> p s k", s=T)
                b0 = 4 * (c % 2)
                nc.vector.tensor_copy(o[:, :, 0:CCH], ps[:, b0 + 2, 0:CTX].rearrange("p (k s) -> p s k", s=T))
                z = ps[:, b0:b0 + 2, :].rearrange("p b (k s) -> p s (b k)", s=T)
                nc.vector.tensor_copy(o[:, :, CCH:CH], z).then_inc(conv, 1)

    tr, ev = k.sem("v_tr"), k.sem("v_ev")
    with nc.Block() as block:
        @block.tensor
        def _(pe):
            for n in range(16):
                which, j = n % 2, n // 2
                if n >= 4:
                    pe.wait_ge(ev, n - 3)
                for q in range(HQ):
                    src = z_t[:, which * HQ + q, :].rearrange("p (t r) -> p r t", r=2)[:, j // 4, (j % 4) * P:(j % 4 + 1) * P]
                    last = nc.tensor.transpose(ps[:, n % 4, q * P:(q + 1) * P], src, k.ident)
                last.then_inc(tr, 1)

        @block.vector
        def _(dve):
            for n in range(16):
                which, j = n % 2, n // 2
                dve.wait_ge(tr, n + 1)
                if which:
                    nc.vector.tensor_tensor(k.x1[:, j, :], ps[:, n % 4, :], k.inv_row, ALU.mult).then_inc(ev, 1)
                else:
                    nc.vector.tensor_copy(k.v[:, j, :], ps[:, n % 4, :]).then_inc(ev, 1)


def filters(k, order):
    nc, ps = k.nc, k.ps
    tag = f"f{order}_"
    sd = k.greg.rearrange("p (w j c) -> p w j c", w=2, j=8)
    w1 = k.tmp[0:FEATS, 0:FW]
    w2 = k.tmp[0:FW, 64:128]
    vec = k.tmp[0:FW, 128:136]
    feats = k.at(120, 4)[0:FEATS, :]
    w3 = k.at(124, 8)[0:FW, 0:2 * HY]
    b3 = k.at(128, 4)[0:1, :]
    decay = k.at(132, 16).rearrange("p (j c) -> p j c", j=8)
    hid = [k.tmp[0:FW, 256 + i * SEQ:256 + (i + 1) * SEQ] for i in range(3)]
    fb = k.tmp[:, 3584:3584 + 4 * HY].rearrange("p (w c) -> p w c", w=4)
    hyb = k.extra[0:1, 0:HY]
    ab = k.at(64, 8).rearrange("p (b w c) -> p b w c", b=2, w=2)
    absd = k.sem(tag + "abs")
    acc = k.extra[:, HY:2 * HY]
    loaded, mm, sv, own, kf, pss, sine = k.sem(tag + "load"), k.sem(tag + "mm"), k.sem(tag + "scale"), k.sem(tag + "own"), k.sem(tag + "k"), k.sem(tag + "norm"), k.sem(tag + "sine")
    hready = k.sem(tag + "h")

    with nc.Block() as block:
        @block.sync
        def _(sp):
            n = 0
            for ap, src in ((w1, k.i["hy_w1"][0]), (w2, k.i["hy_w2"][0]), (feats, k.c["feats_t"]),
                            (vec[:, 0:1], k.i["hy_b1"].rearrange("l n -> n l")), (vec[:, 1:2], k.i["hy_b2"].rearrange("l n -> n l")),
                            (vec[:, 2:3], k.i["hy_freq"][0, 0:1].rearrange("l n -> n l")), (vec[:, 3:4], k.i["hy_freq"][0, 1:2].rearrange("l n -> n l")),
                            (w3, k.i["hy_w3"][0, :, order * 2 * HY:(order + 1) * 2 * HY]), (b3, k.i["hy_b3"][:, order * 2 * HY:(order + 1) * 2 * HY]),
                            (decay, k.c["decay"]), (hyb, k.i["hy_bias"][0, order:order + 1, :])):
                sp.dma_start(ap, src).then_inc(loaded, 16)
            sp.wait_ge(loaded, 11 * 16)

        @block.tensor
        def _(pe):
            pe.wait_ge(loaded, 11 * 16)
            for layer in range(2):
                for h in range(2):
                    if layer:
                        pe.wait_ge(sine, 1)
                        nc.tensor.matmul(ps[0:FW, 2 + h, :], w2, hid[2][:, h * 512:(h + 1) * 512], start=True, stop=True).then_inc(mm, 1)
                    else:
                        nc.tensor.matmul(ps[0:FW, h, :], w1, feats[:, h * 512:(h + 1) * 512], start=True, stop=True).then_inc(mm, 1)
            pe.wait_ge(sine, 2)
            for j in range(8):
                if j >= 2:
                    pe.wait_ge(kf, j - 1)
                for d in range(2):
                    o = ps[:, 4 + 2 * (j % 2) + d, :]
                    nc.tensor.matmul(o, hid[2][:, j * P:(j + 1) * P], w3[:, d * HY:(d + 1) * HY], start=True, stop=False)
                    last = nc.tensor.matmul(o, k.ones[0:1, :], b3[:, d * HY:(d + 1) * HY], start=False, stop=True)
                last.then_inc(mm, 1)
            pe.wait_ge(pss, 15)
            nc.tensor.matmul(ps[:, 0, :], k.ones, acc, start=True, stop=True)
            for q in range(HQ):
                last = nc.tensor.matmul(ps[:, 1, q:q + 1], acc[:, q * P:(q + 1) * P], k.ones[:, 0:1], start=True, stop=True)
            last.then_inc(mm, 1)

        @block.gpsimd
        def _(pool):
            for j in range(8):
                pool.wait_ge(absd, j + 1)
                if j == 0:
                    nc.gpsimd.tensor_tensor(acc, ab[:, 0, 0, :], ab[:, 0, 1, :], ALU.add).then_inc(pss, 1)
                    pool.wait_ge(pss, 1)
                else:
                    for w in range(2):
                        nc.gpsimd.tensor_tensor(acc, acc, ab[:, j % 2, w, :], ALU.add).then_inc(pss, 1)
                        pool.wait_ge(pss, 2 * j + w)

        @block.scalar
        def _(act):
            for layer in range(2):
                act.wait_ge(hready, layer + 1)
                nc.scalar.activation(hid[2], hid[1], ACT.Sin, scale=TURN).then_inc(sine, 1)
            for j in range(8):
                act.wait_ge(kf, j + 1)
                if j >= 2:
                    act.wait_ge(pss, 2 * j - 3)
                nc.scalar.activation(ab[:, j % 2], fb[:, 2 * (j % 2):2 * (j % 2) + 2, :], ACT.Abs).then_inc(absd, 1)

        @block.vector
        def _(dve):
            link = Links(dve, own)
            dve.wait_ge(loaded, 11 * 16)
            link(nc.vector.tensor_scalar(vec[:, 4:6], vec[:, 2:4], INV_TURN, None, ALU.mult))
            for layer in range(2):
                dve.wait_ge(mm, 2 * layer + 2)
                z = ps[0:FW, 2 * layer:2 * layer + 2, :].rearrange("p b n -> p (b n)")
                link(nc.vector.tensor_scalar(hid[0], z, vec[:, layer:layer + 1], vec[:, 4 + layer:5 + layer], ALU.add, ALU.mult))
                link(nc.vector.tensor_scalar(hid[1], hid[0], ROUND, ROUND, ALU.add, ALU.subtract))
                nc.vector.tensor_tensor(hid[1], hid[0], hid[1], ALU.subtract).then_inc(hready, 1)
            for j in range(8):
                dve.wait_ge(mm, 4 + j + 1)
                b = 4 + 2 * (j % 2)
                s, d = sd[:, 0, j, :], sd[:, 1, j, :]
                fw, bw = fb[:, 2 * (j % 2), :], fb[:, 2 * (j % 2) + 1, :]
                if j >= 2:
                    dve.wait_ge(absd, j - 1)
                nc.vector.tensor_tensor(fw, ps[:, b, :], decay[:, j, :], ALU.mult)
                link(nc.vector.tensor_tensor(bw, ps[:, b + 1, :], decay[:, j, :], ALU.mult))
                if j == 0:
                    link(nc.vector.memset(fb[0:1, 1, :], 0.0))
                nc.vector.tensor_tensor(s, fw, bw, ALU.add)
                nc.vector.tensor_tensor(d, bw, fw, ALU.subtract).then_inc(kf, 1)
            dve.wait_ge(mm, 13)
            dve.wait_ge(kf, 8)
            dve.wait_ge(absd, 8)
            link(nc.vector.tensor_tensor(fb[0:1, 2, :], hyb, ps[0:1, 0, :], ALU.mult))
            nc.vector.tensor_tensor(sd[0:1, 0, 0, :], sd[0:1, 0, 0, :], fb[0:1, 2, :], ALU.add)
            nc.vector.reciprocal(k.inv_row, ps[:, 0, :])
            nc.vector.reciprocal(k.inv_col, ps[:, 1, 0:HQ])

    ring = [k.sem(tag + f"ring{s}") for s in range(4)]
    mm2, cp, own2, done = k.sem(tag + "mm2"), k.sem(tag + "cp"), k.sem(tag + "own2"), k.sem(tag + "done")
    half = k.tmp[:, 0:4 * HY].rearrange("p (b w c) -> p b w c", b=2, w=2)
    with nc.Block() as block:
        @block.sync
        def _(sp):
            for f in range(4):
                sp.dma_start(k.ring[:, f, :], k.c["dft_filter"][f].rearrange("p m k n -> p (m k n)")).then_inc(ring[f], 16)

        @block.tensor
        def _(pe):
            for f in range(4):
                pe.wait_ge(ring[f], 16)
                if f >= 2:
                    pe.wait_ge(done, f - 1)
                m = k.ring[:, f, :].rearrange("p (m k n) -> p m k n", m=4, k=4)
                for mat in range(4):
                    for kk in range(4):
                        last = nc.tensor.matmul(ps[:, 4 * (f % 2) + mat, :], m[:, mat, kk, :], sd[:, mat // 2, 4 * (mat % 2) + kk, :], start=kk == 0, stop=kk == 3)
                last.then_inc(mm2, 1)

        @block.scalar
        def _(act):
            for f in range(4):
                act.wait_ge(mm2, f + 1)
                if f >= 2:
                    act.wait_ge(done, f - 1)
                nc.scalar.activation(half[:, f % 2, 0, :], ps[:, 4 * (f % 2) + 1, :], ACT.Copy)
                nc.scalar.activation(half[:, f % 2, 1, :], ps[:, 4 * (f % 2) + 3, :], ACT.Copy).then_inc(cp, 1)

        @block.vector
        def _(dve):
            for f in range(4):
                dve.wait_ge(cp, f + 1)
                b = 4 * (f % 2)
                co, so = half[:, f % 2, 0, :], half[:, f % 2, 1, :]
                nc.vector.tensor_tensor(k.spec[:, 0, f, :], ps[:, b, :], co, ALU.add)
                nc.vector.tensor_tensor(k.spec[:, 1, f, :], ps[:, b + 2, :], so, ALU.add)
                nc.vector.tensor_tensor(k.spec[:, 2, f, :], ps[:, b, :], co, ALU.subtract)
                nc.vector.tensor_tensor(k.spec[:, 3, f, :], so, ps[:, b + 2, :], ALU.subtract).then_inc(done, 1)


def long_conv(k, order):
    nc, ps = k.nc, k.ps
    tag = f"l{order}_"
    g = k.greg.rearrange("p (a f c) -> p a f c", a=4, f=4)
    ring = [k.sem(tag + f"ring{s}") for s in range(4)]
    half = k.at(152, 8).rearrange("p (b w c) -> p b w c", b=2, w=2)
    u = k.at(160, 16).rearrange("p (w c) -> p w c", w=8)
    mm, cp, own, done, inv, fin = k.sem(tag + "mm"), k.sem(tag + "cp"), k.sem(tag + "own"), k.sem(tag + "done"), k.sem(tag + "inv"), k.sem(tag + "fin")
    with nc.Block() as block:
        @block.sync
        def _(sp):
            for f in range(4):
                sp.dma_start(k.ring[:, f, :], k.c["dft_signal"][f].rearrange("p m k n -> p (m k n)")).then_inc(ring[f], 16)
            for i in range(4):
                sp.wait_ge(mm, i + 1)
                sp.dma_start(k.ring[:, i, :], k.c["dft_inverse"][i].rearrange("p k n -> p (k n)")).then_inc(ring[i], 16)

        @block.tensor
        def _(pe):
            for f in range(4):
                pe.wait_ge(ring[f], 16)
                if f >= 2:
                    pe.wait_ge(done, f - 1)
                m = k.ring[:, f, :].rearrange("p (m k n) -> p m k n", m=4, k=4)
                for mat in range(4):
                    for kk in range(4):
                        last = nc.tensor.matmul(ps[:, 4 * (f % 2) + mat, :], m[:, mat, kk, :], k.v[:, 4 * (mat % 2) + kk, :], start=kk == 0, stop=kk == 3)
                last.then_inc(mm, 1)
            pe.wait_ge(done, 4)
            for n in range(8):
                par, tile = divmod(n, 4)
                if n % 4 == 0:
                    pe.wait_ge(ring[2 * par], 32)
                    pe.wait_ge(ring[2 * par + 1], 32)
                if n >= 4:
                    pe.wait_ge(fin, n - 3)
                for cs in range(2):
                    m = k.ring[:, 2 * par + cs, :].rearrange("p (k n) -> p k n", k=4)
                    for kk in range(4):
                        a, b = m[:, kk, :], g[:, 2 * par + cs, kk, :]
                        a, b = (a[:, tile * P:(tile + 1) * P], b) if order == 0 else (b[:, tile * P:(tile + 1) * P], a)
                        last = nc.tensor.matmul(ps[:, n % 4, :], a, b, start=cs + kk == 0, stop=cs == 1 and kk == 3)
                last.then_inc(inv, 1)

        @block.scalar
        def _(act):
            for f in range(4):
                act.wait_ge(mm, f + 1)
                if f >= 2:
                    act.wait_ge(done, f - 1)
                nc.scalar.activation(half[:, f % 2, 0, :], ps[:, 4 * (f % 2) + 1, :], ACT.Copy)
                nc.scalar.activation(half[:, f % 2, 1, :], ps[:, 4 * (f % 2) + 3, :], ACT.Copy).then_inc(cp, 1)

        @block.vector
        def _(dve):
            link = Links(dve, own)
            tt = nc.vector.tensor_tensor
            for f in range(4):
                dve.wait_ge(cp, f + 1)
                b = 4 * (f % 2)
                co, so = half[:, f % 2, 0, :], half[:, f % 2, 1, :]
                re, um, reb, umb = (u[:, i, :] for i in range(4))
                tt(re, ps[:, b, :], co, ALU.add)
                tt(umb, ps[:, b, :], co, ALU.subtract)
                tt(um, ps[:, b + 2, :], so, ALU.add)
                link(tt(reb, ps[:, b + 2, :], so, ALU.subtract))
                for bar, (a, m) in enumerate(((re, um), (reb, umb))):
                    kre, kim = k.spec[:, 2 * bar, f, :], k.spec[:, 2 * bar + 1, f, :]
                    t0, t1, t2, t3 = (u[:, 4 + i, :] for i in range(4))
                    tt(t0, a, kre, ALU.mult)
                    tt(t1, m, kim, ALU.mult)
                    tt(t2, m, kre, ALU.mult)
                    link(tt(t3, a, kim, ALU.mult))
                    tt(a, t0, t1, ALU.add)
                    link(tt(m, t2, t3, ALU.subtract))
                tt(g[:, 0, f, :], re, umb, ALU.add)
                tt(g[:, 1, f, :], um, reb, ALU.add)
                tt(g[:, 2, f, :], re, umb, ALU.subtract)
                tt(g[:, 3, f, :], um, reb, ALU.subtract).then_inc(done, 1)
                dve.wait_ge(done, f + 1)
            for n in range(8):
                par, tile = divmod(n, 4)
                dve.wait_ge(inv, n + 1)
                if order == 0:
                    tt(k.v[:, n, :], ps[:, n % 4, :], k.x1[:, n, :], ALU.mult).then_inc(fin, 1)
                else:
                    o = k.x2t[:, tile, :].rearrange("p (t r) -> p r t", r=2)[:, par, :]
                    nc.vector.scalar_tensor_tensor(o, ps[:, n % 4, :], k.inv_col[:, tile:tile + 1], o, ALU.mult, ALU.mult).then_inc(fin, 1)


def s5(k):
    nc, ps = k.nc, k.ps
    NC = 2 * PAIRS
    cos = k.at(0, 10).rearrange("p (c j) -> p c j", j=CH)
    sin = k.at(10, 10).rearrange("p (c j) -> p c j", j=CH)
    dec = k.at(20, 10).rearrange("p (c j) -> p c j", j=CH)
    bre = k.at(48, 10).rearrange("p (c j) -> p c j", j=CH)
    bim = k.at(58, 10).rearrange("p (c j) -> p c j", j=CH)
    t1 = k.at(68, 10).rearrange("p (c j) -> p c j", j=CH)
    t2 = k.at(78, 10).rearrange("p (c j) -> p c j", j=CH)
    ep = k.at(68, 16).rearrange("p (r d a n) -> p r d a n", r=2, d=2, a=8)
    et = k.at(88, 16).rearrange("p (r d a n) -> p r d a n", r=2, d=2, a=8)
    ot = k.at(104, 16).rearrange("p (r d a n) -> p r d a n", r=2, d=2, a=8)
    ll = k.at(120, 8).rearrange("p (a w n) -> p a w n", a=8, w=2)
    uc = k.at(128, 10).rearrange("p (g j) -> p g j", j=CH)
    ys = k.at(138, 8).rearrange("p (g j) -> p g j", j=XCH)
    lw = k.at(146, 8)[0:32, 0:8 * 240].rearrange("p (a n) -> p a n", a=8)
    tmp = k.at(154, 22)
    pre = tmp[:, 0:576].rearrange("p (c e) -> p c e", e=NEXP)
    pim = tmp[:, 576:1152].rearrange("p (c e) -> p c e", e=NEXP)
    bd = tmp[:, 1152:1152 + 2048].rearrange("p (r c w h) -> p r c w h", r=2, c=NC, w=2)
    ct = tmp[:, 3200:3200 + 1024].rearrange("p (r c h) -> p r c h", r=2, c=NC)
    par = k.extra
    rows = k.at(48, 1)[0:96, 0:P]
    braw = k.at(50, 4).rearrange("p (r c h) -> p r c h", r=2, c=NC)
    craw = k.at(54, 4).rearrange("p (r d q n) -> p r d q n", r=2, d=2, q=2)
    step = k.at(30, 2)[:, 0:NEXP + CH]
    bbar = k.at(154 + 18, 4).rearrange("p (r c h) -> p r c h", r=2, c=NC)
    lt = par[:, 0:96]
    dt, xr, tau = par[:, 96:128], par[:, 128:160], par[:, 160:192]
    tau8, r8, mm_, q0, q1, w0_, w1_ = (par[:, 192 + 32 * i:224 + 32 * i] for i in range(7))
    cneg = par[:, 512:1024].rearrange("p (c h) -> p c h", c=NC)
    sc = [k.at(58 + 3 * i, 3)[:, 0:576].rearrange("p (c e) -> p c e", e=NEXP) for i in range(3)]
    sb = [k.at(70 + 2 * i, 2).rearrange("p (c h) -> p c h", c=NC) for i in range(2)]

    loaded, turned, own, aready, adone, pz, spread, bdz = (k.sem("s_" + n) for n in ("load", "turned", "own", "aready", "adone", "pz", "spread", "bdz"))
    with nc.Block() as block:
        @block.sync
        def _(sp):
            sp.dma_start(rows[0:32, :], k.i["s5_lam_re"].rearrange("l d (a w) p -> (l d a) (w p)", w=2)).then_inc(loaded, 16)
            sp.dma_start(rows[32:64, :], k.i["s5_lam_im"].rearrange("l d (a w) p -> (l d a) (w p)", w=2)).then_inc(loaded, 16)
            sp.dma_start(rows[64:96, 0:2], k.i["s5_log_step"].rearrange("l d (a w) -> (l d a) w", w=2)).then_inc(loaded, 16)
            sp.dma_start(step, k.c["steps"]).then_inc(loaded, 16)
            for r, name in enumerate(("s5_b_re", "s5_b_im")):
                for d in range(2):
                    sp.dma_start(braw[:, r, d * PAIRS:(d + 1) * PAIRS, :], k.i[name][0, d].rearrange("(a w) p h -> (w p) a h", w=2)).then_inc(loaded, 16)
            for r, name in enumerate(("s5_c_re", "s5_c_im")):
                for d in range(2):
                    for q in range(2):
                        for a in range(8):
                            src = k.i[name][0, d, 16 * q + 2 * a:16 * q + 2 * a + 2].rearrange("w h p -> h w p")
                            sp.dma_start(craw[16 * a:16 * a + 16, r, d, q, :].rearrange("h (w p) -> h w p", w=2), src).then_inc(loaded, 16)

        NL = (4 + 4 + 64) * 16

        @block.gpsimd
        def _(pool):
            nc.gpsimd.memset(bd, 0.0).then_inc(bdz, 1)

        @block.tensor
        def _(pe):
            pe.wait_ge(loaded, NL)
            pe.wait_ge(spread, 1)
            nc.tensor.transpose(ps[:, 0, 0:96], rows, k.ident[0:96, 0:96]).then_inc(turned, 1)
            for r in range(2):
                for d in range(2):
                    for q in range(2):
                        n = 4 * r + 2 * d + q
                        last = nc.tensor.transpose(ps[:, 1 + n // 4, (n % 4) * P:(n % 4 + 1) * P], craw[:, r, d, q, :], k.ident)
            last.then_inc(turned, 1)

        @block.scalar
        def _(act):
            act.wait_ge(aready, 1)
            nc.scalar.activation(dt, lt[:, 64:96], ACT.Exp).then_inc(adone, 1)
            act.wait_ge(aready, 2)
            nc.scalar.activation(sc[0], sc[0], ACT.Exp).then_inc(adone, 1)
            act.wait_ge(aready, 3)
            nc.scalar.activation(sc[1], sc[1], ACT.Sin, scale=TURN)
            nc.scalar.activation(sc[2], sc[2], ACT.Sin, scale=TURN).then_inc(adone, 1)

        @block.vector
        def _(dve):
            link = Links(dve, own)
            tt, ts = nc.vector.tensor_tensor, nc.vector.tensor_scalar
            dve.wait_ge(loaded, NL)
            link(nc.vector.tensor_copy(sb[0][64:96, 0, 0:2], rows[64:96, 0:2]))
            nc.vector.tensor_copy(rows[64:96, :].rearrange("p (w n) -> p w n", w=2), bcast(sb[0][64:96, 0, 0:2], [32, 2, NP])).then_inc(spread, 1)
            dve.wait_ge(turned, 2)
            nc.vector.tensor_copy(lt, ps[:, 0, 0:96]).then_inc(aready, 1)
            link(nc.vector.tensor_copy(ct.rearrange("p r c h -> p (r c h)"), ps[:, 1:3, :].rearrange("p b n -> p (b n)")))
            ts(cneg, ct[:, 1], -1.0, None, ALU.mult)
            dve.wait_ge(adone, 1)
            tt(xr, lt[:, 0:32], dt, ALU.mult)
            link(nc.vector.scalar_tensor_tensor(tau, lt[:, 32:64], INV_TURN, dt, ALU.mult, ALU.mult))
            e = step[:, 0:NEXP].unsqueeze(1).to_broadcast([P, NC, NEXP])
            tt(sc[0], bcast(xr, [P, NC, NEXP]), e, ALU.mult).then_inc(aready, 1)
            link(tt(sc[1], bcast(tau, [P, NC, NEXP]), e, ALU.mult))
            link(ts(sc[2], sc[1], 0.25, None, ALU.add))
            for s in (sc[1], sc[2]):
                link(ts(pre, s, ROUND, ROUND, ALU.add, ALU.subtract))
                link(tt(s, s, pre, ALU.subtract))
            ts(w0_, tau, float(T), None, ALU.mult).then_inc(aready, 1)
            dve.wait_ge(aready, 3)
            link(ts(w1_, w0_, ROUND, ROUND, ALU.add, ALU.subtract))
            tt(tau8, w0_, w1_, ALU.subtract)
            dve.wait_ge(adone, 3)
            tt(pre, sc[0], sc[2], ALU.mult)
            link(tt(pim, sc[0], sc[1], ALU.mult))
            nc.vector.tensor_copy(r8, sc[0][:, :, T])
            lr, li = lt[:, 0:32], lt[:, 32:64]
            link(ts(w0_, pre[:, :, 1], -1.0, None, ALU.add))
            b1 = pim[:, :, 1]
            link(tt(q0, w0_, lr, ALU.mult))
            link(tt(w1_, b1, li, ALU.mult))
            link(tt(q0, q0, w1_, ALU.add))
            link(tt(q1, b1, lr, ALU.mult))
            link(tt(w1_, w0_, li, ALU.mult))
            link(tt(q1, q1, w1_, ALU.subtract))
            link(tt(mm_, lr, lr, ALU.mult))
            link(tt(w1_, li, li, ALU.mult))
            link(tt(mm_, mm_, w1_, ALU.add))
            link(nc.vector.reciprocal(mm_, mm_))
            tt(q0, q0, mm_, ALU.mult)
            link(tt(q1, q1, mm_, ALU.mult))
            Q0, Q1 = bcast(q0, [P, NC, NH]), bcast(q1, [P, NC, NH])
            tt(bbar[:, 0], braw[:, 0], Q0, ALU.mult)
            tt(bbar[:, 1], braw[:, 0], Q1, ALU.mult)
            tt(sb[0], braw[:, 1], Q1, ALU.mult)
            link(tt(sb[1], braw[:, 1], Q0, ALU.mult))
            tt(bbar[:, 0], bbar[:, 0], sb[0], ALU.subtract)
            link(tt(bbar[:, 1], bbar[:, 1], sb[1], ALU.add))
            dve.wait_ge(bdz, 1)
            for w in range(2):
                p = slice(NP * w, NP * w + NP)
                nc.vector.tensor_copy(bd[p, :, :, w, :], bbar[p])

    for hh in range(2):
        s5_half(k, hh, locals())


def s5_half(k, hh, b):
    nc, ps = k.nc, k.ps
    cos, sin, dec, bre, bim, t1, t2, ep, et, ot, ll, uc, ys, lw = (b[n] for n in "cos sin dec bre bim t1 t2 ep et ot ll uc ys lw".split())
    pre, pim, bd, ct, cneg, bbar, step, tau8, r8 = (b[n] for n in "pre pim bd ct cneg bbar step tau8 r8".split())
    tag = f"h{hh}_"
    S = lambda n: k.sem(tag + n)
    ugot, own, osem, pown, tr, ev, lmm, lev, lput = (S(n) for n in ("u", "own", "o", "pown", "tr", "ev", "lmm", "lev", "lput"))
    epd, ang, trig = S("ep"), S("ang"), S("trig")
    t3, t4 = k.at(20, 4), k.at(24, 4)
    pt = k.at(48, 8)

    def table(tt, link, out, cre, cim, first, sign, s0, s1):
        for d in range(2):
            cols = slice(d * PAIRS + 8 * hh, d * PAIRS + 8 * hh + 8)
            e = slice(first[d], first[d] + T)
            shape = [P, 8, T, NH]
            pr, pi = bcast(pre[:, cols, e], shape), bcast(pim[:, cols, e], shape)
            cr, ci = (x[:, cols, :].unsqueeze(2).to_broadcast(shape) for x in (cre, cim))
            o = [out[:, r, d].rearrange("p a (s h) -> p a s h", h=NH) for r in range(2)]
            m0, m1 = (x.rearrange("p (a s h) -> p a s h", a=8, h=NH) for x in (s0, s1))
            tt(o[0], cr, pr, ALU.mult)
            tt(o[1], cr, pi, ALU.mult)
            tt(m0, ci, pi, ALU.mult)
            link(tt(m1, ci, pr, ALU.mult))
            tt(o[0], o[0], m0, ALU.subtract)
            link(tt(o[1], o[1], m1, ALU.add))
            if sign < 0:
                link((nc.gpsimd if tt == nc.gpsimd.tensor_tensor else nc.vector).tensor_scalar(out[:, 1, d], out[:, 1, d], -1.0, None, ALU.mult))

    with nc.Block() as block:
        @block.sync
        def _(sp):
            src = k.z_u.rearrange("(g h) s j -> s h g j", h=NH)
            for s in range(T):
                sp.dma_start(uc[NH * s:NH * s + NH, :, :], src[s, :, 16 * hh:16 * hh + 16, :]).then_inc(ugot, 16)
            sp.wait_ge(lev, 8)
            for s in range(T):
                for w in range(2):
                    sp.dma_start(ll[NH * s:NH * s + NH, :, w, :], lw[NH * w:NH * w + NH, :, (T - 1 - s) * NH:(T - 1 - s) * NH + P]).then_inc(lput, 16)
            sp.wait_ge(lput, 256)
            sp.wait_ge(ugot, 128)

        @block.vector
        def _(dve):
            link = Links(dve, own)
            table(nc.vector.tensor_tensor, link, ep, bbar[:, 0], bbar[:, 1], (T + 2, 0), 1, t3, t4)
            nc.vector.tensor_copy(t3[:, 0:1], t4[:, 0:1]).then_inc(epd, 1)
            for i in range(8):
                dve.wait_ge(tr, i + 1)
                r, d, a = i // 4, (i // 2) % 2, 4 * (i % 2)
                nc.vector.tensor_copy(et[:, r, d, a:a + 4, :], ps[:, i % 4, :].rearrange("p (a n) -> p a n", a=4)).then_inc(ev, 1)
            for a in range(8):
                dve.wait_ge(lmm, a + 1)
                nc.vector.tensor_copy(lw[:, a, :], ps[0:32, 4 + a % 2, 0:240]).then_inc(lev, 1)

        @block.gpsimd
        def _(pool):
            link = Links(pool, pown)
            table(nc.gpsimd.tensor_tensor, link, ot, ct[:, 0], ct[:, 1], (1, T + 1), -1, pt[:, 0:1024], pt[:, 1024:2048])
            nc.gpsimd.memset(pt[:, 0:1], 0.0).then_inc(osem, 1)

        @block.tensor
        def _(pe):
            pe.wait_ge(epd, 1)
            for i in range(8):
                r, d, a = i // 4, (i // 2) % 2, 4 * (i % 2)
                if i >= 4:
                    pe.wait_ge(ev, i - 3)
                for x in range(4):
                    last = nc.tensor.transpose(ps[:, i % 4, x * P:(x + 1) * P], ep[:, r, d, a + x, :], k.ident)
                last.then_inc(tr, 1)
            pe.wait_ge(osem, 1)
            for a in range(8):
                if a >= 2:
                    pe.wait_ge(lev, a - 1)
                o = ps[0:32, 4 + a % 2, :]
                lhs = lambda r, d: bd[:, r, d * PAIRS + 8 * hh + a].rearrange("p w h -> p (w h)")
                for r in range(2):
                    nc.tensor.matmul(o[:, 0:112], lhs(r, 1), ot[:, r, 1, a, NH:P], start=r == 0, stop=r == 1)
                for i, (r, d) in enumerate(((0, 0), (1, 0), (0, 1), (1, 1))):
                    c = (ct[:, 0], cneg)[r]
                    nc.tensor.matmul(o[:, 112:128], lhs(r, d), c[:, d * PAIRS + 8 * hh + a, :], start=i == 0, stop=i == 3)
                for r in range(2):
                    last = nc.tensor.matmul(o[:, 128:240], lhs(r, 0), ot[:, r, 0, a, 0:112], start=r == 0, stop=r == 1)
                last.then_inc(lmm, 1)

    smm, sev, angs, sins, own2, omm, oev, yput, scd = (S(n) for n in ("smm", "sev", "angs", "sins", "own2", "omm", "oev", "yput", "scan"))
    with nc.Block() as block:
        @block.tensor
        def _(pe):
            for c in range(16):
                d, a = divmod(c, 8)
                if c >= 4:
                    pe.wait_ge(sev, c - 3)
                for w in range(2):
                    u = uc[:, 2 * a + w, :]
                    for r in range(2):
                        o = ps[NP * w:NP * w + NP, c % 4, r * CH:(r + 1) * CH]
                        lhs = et[:, r, d, a, NP * w:NP * w + NP]
                        if d == 0:
                            last = nc.tensor.matmul(o, lhs, u, start=True, stop=True)
                        else:
                            nc.tensor.matmul(o[:, 0:CCH], lhs, u[:, CCH - 1::-1], start=True, stop=True)
                            last = nc.tensor.matmul(o[:, CCH:CH], lhs, u[:, CH - 1:CCH - 1:-1], start=True, stop=True)
                last.then_inc(smm, 1)
            pe.wait_ge(scd, 1)
            for n in range(4):
                for x in range(4):
                    h4, w = divmod(n, 2)
                    a = 4 * h4 + x
                    gi = 2 * a + w
                    p = slice(NP * w, NP * w + NP)
                    o = ps[:, 4 + n, x * P:(x + 1) * P]
                    nc.tensor.matmul(o, ll[:, a, w, :], uc[:, gi, CCH:CH], start=True, stop=False)
                    for r, st in enumerate((t1, t2)):
                        nc.tensor.matmul(o, ot[p, r, 0, a, :], st[p, a, CCH - 1:CH - 1], start=False, stop=False)
                        last = nc.tensor.matmul(o, ot[p, r, 1, a, :], st[p, 8 + a, CH - 2:CCH - 2:-1], start=False, stop=r == 1)
                last.then_inc(omm, 1)

        @block.scalar
        def _(act):
            act.wait_ge(angs, 1)
            nc.scalar.activation(sin, sin, ACT.Sin, scale=TURN).then_inc(sins, 1)
            act.wait_ge(angs, 2)
            nc.scalar.activation(cos, cos, ACT.Sin, scale=TURN).then_inc(sins, 1)
            for c in range(16):
                act.wait_ge(smm, c + 1)
                nc.scalar.activation(bre[:, c, :], ps[:, c % 4, 0:CH], ACT.Copy)
                nc.scalar.activation(bim[:, c, :], ps[:, c % 4, CH:2 * CH], ACT.Copy).then_inc(sev, 1)
            for n in range(4):
                act.wait_ge(omm, n + 1)
                h4, w = divmod(n, 2)
                nc.scalar.activation(ys.rearrange("p (a w) j -> p w a j", w=2)[:, w, 4 * h4:4 * h4 + 4, :], ps[:, 4 + n, :].rearrange("p (g j) -> p g j", g=4), ACT.Copy).then_inc(oev, 1)

        @block.vector
        def _(dve):
            link = Links(dve, own2)
            tt, ts = nc.vector.tensor_tensor, nc.vector.tensor_scalar
            for d in range(2):
                cols = slice(d * PAIRS + 8 * hh, d * PAIRS + 8 * hh + 8)
                link(tt(sin[:, 8 * d:8 * d + 8, :], bcast(tau8[:, cols], [P, 8, CH]), step[:, NEXP:NEXP + CH].unsqueeze(1).to_broadcast([P, 8, CH]), ALU.mult))
                nc.vector.tensor_copy(dec[:, 8 * d:8 * d + 8, :], bcast(r8[:, cols], [P, 8, CH]))
            link(ts(t1, sin, ROUND, ROUND, ALU.add, ALU.subtract))
            link(tt(sin, sin, t1, ALU.subtract))
            link(ts(cos, sin, 0.25, None, ALU.add))
            link(ts(t1, cos, ROUND, ROUND, ALU.add, ALU.subtract))
            tt(cos, cos, t1, ALU.subtract).then_inc(angs, 1)
            nc.vector.memset(dec[:, :, 0:1], 0.0).then_inc(angs, 1)
            dve.wait_ge(sins, 2)
            dve.wait_ge(sev, 16)
            tt(t1, bre, cos, ALU.mult)
            link(tt(t2, bim, sin, ALU.mult))
            link(tt(t1, t1, t2, ALU.add))
            tt(t2, bim, cos, ALU.mult)
            link(tt(bre, bre, sin, ALU.mult))
            link(tt(t2, t2, bre, ALU.subtract))
            flat = lambda x: x.rearrange("p c j -> p (c j)")
            nc.vector.tensor_tensor_scan(flat(bre), flat(dec), flat(t1), 0.0, ALU.mult, ALU.add)
            link(nc.vector.tensor_tensor_scan(flat(bim), flat(dec), flat(t2), 0.0, ALU.mult, ALU.add))
            tt(t1, bre, cos, ALU.mult)
            link(tt(t2, bim, sin, ALU.mult))
            link(tt(t1, t1, t2, ALU.subtract))
            tt(t2, bre, sin, ALU.mult)
            link(tt(bim, bim, cos, ALU.mult))
            tt(t2, t2, bim, ALU.add).then_inc(scd, 1)

        @block.sync
        def _(sp):
            sp.wait_ge(oev, 4)
            dst = k.z_y.rearrange("(g h) t j -> t h g j", h=NH)
            for t in range(T):
                sp.dma_start(dst[t, :, 16 * hh:16 * hh + 16, :], ys[NH * t:NH * t + NH, :, :]).then_inc(yput, 16)
            sp.wait_ge(yput, 128)


def glu_and_out(k):
    nc, ps = k.nc, k.ps
    yl = k.at(0, 16).rearrange("p (q n) -> p q n", q=4)
    ul = k.at(16, 16).rearrange("p (q n) -> p q n", q=4)
    gw = k.at(48, 8).rearrange("p (q n) -> p q n", q=4)
    y5 = k.at(56, 16).rearrange("p (q n) -> p q n", q=4)
    sg = k.at(72, 8).rearrange("p (s n) -> p s n", s=4)
    wo = k.at(80, 32).rearrange("p (k n) -> p k n", k=KD)
    x2 = k.x2v
    loaded, pre, gel, mm, sig, fin, got, omm, own, xg, wgot = (k.sem("g_" + n) for n in ("load", "pre", "gelu", "mm", "sig", "fin", "got", "omm", "own", "x", "w"))
    with nc.Block() as block:
        @block.sync
        def _(sp):
            sp.dma_start(yl, k.z_y.rearrange("(q p) t j -> p q (t j)", p=P)).then_inc(loaded, 16)
            for q in range(4):
                sp.dma_start(ul[:, q, :].rearrange("p (t j) -> p t j", t=T), k.z_u[q * P:(q + 1) * P, :, CCH:CH]).then_inc(loaded, 16)
            sp.dma_start(gw, k.i["s5_glu_w"].rearrange("l (q p) n -> p (l q) n", p=P)).then_inc(wgot, 16)
            sp.dma_start(wo, k.i["w_out"].rearrange("l (q p) n -> p (l q) n", p=P)).then_inc(wgot, 16)
            sp.dma_start(x2, k.i["x"].rearrange("b (m p) n -> p (b m) n", p=P)).then_inc(xg, 16)

        @block.vector
        def _(dve):
            link = Links(dve, own)
            dve.wait_ge(loaded, 80)
            r = ROWS["d"][0]
            for q in range(4):
                nc.vector.scalar_tensor_tensor(yl[:, q, :], ul[:, q, :], k.cols[:, r + q:r + q + 1], yl[:, q, :], ALU.mult, ALU.add).then_inc(pre, 1)
            for n in range(8):
                q, h = divmod(n, 2)
                dve.wait_ge(sig, n + 1)
                o = y5[:, q, :].rearrange("p (j t) -> p t j", t=T)[:, 4 * h:4 * h + 4, :]
                a = yl[:, q, 512 * h:512 * h + 512].rearrange("p (t j) -> p t j", t=4)
                nc.vector.tensor_tensor(o, sg[:, n % 4, :].rearrange("p (t j) -> p t j", t=4), a, ALU.mult).then_inc(fin, 1)
            dve.wait_ge(xg, 16)
            for n in range(16):
                m, h = divmod(n, 2)
                dve.wait_ge(omm, n + 1)
                t = sg[:, n % 4, :]
                if n >= 4:
                    dve.wait_ge(got, n - 3)
                else:
                    dve.wait_ge(fin, 8)
                link(nc.vector.tensor_tensor(t, ps[:, 4 + n % 4, :], k.bc[:, k.G1, h * 512:(h + 1) * 512], ALU.mult))
                nc.vector.tensor_tensor(x2[:, m, h * 512:(h + 1) * 512], x2[:, m, h * 512:(h + 1) * 512], t, ALU.add).then_inc(got, 1)
                dve.wait_ge(got, n + 1)

        @block.scalar
        def _(act):
            for q in range(4):
                act.wait_ge(pre, q + 1)
                nc.scalar.activation(yl[:, q, :], yl[:, q, :], ACT.Gelu_apprx_tanh).then_inc(gel, 1)
            r = ROWS["glu_b"][0]
            for n in range(8):
                q, h = divmod(n, 2)
                act.wait_ge(mm, n + 1)
                if n >= 4:
                    act.wait_ge(fin, n - 3)
                nc.scalar.activation(sg[:, n % 4, :], ps[:, n % 4, :], ACT.Sigmoid, bias=k.cols[:, r + q:r + q + 1]).then_inc(sig, 1)

        @block.tensor
        def _(pe):
            pe.wait_ge(gel, 4)
            pe.wait_ge(wgot, 32)
            for n in range(8):
                q, h = divmod(n, 2)
                if n >= 4:
                    pe.wait_ge(sig, n - 3)
                for kk in range(4):
                    last = nc.tensor.matmul(ps[:, n % 4, :], gw[:, kk, q * P:(q + 1) * P], yl[:, kk, 512 * h:512 * h + 512], start=kk == 0, stop=kk == 3)
                last.then_inc(mm, 1)
            pe.wait_ge(fin, 8)
            for n in range(16):
                m, h = divmod(n, 2)
                if n >= 4:
                    pe.wait_ge(got, n - 3)
                for kk in range(8):
                    src = (k.x2t if kk < 4 else y5)[:, kk % 4, m * P:(m + 1) * P]
                    last = nc.tensor.matmul(ps[:, 4 + n % 4, :], src, wo[:, kk, h * 512:(h + 1) * 512], start=kk == 0, stop=kk == 7)
                last.then_inc(omm, 1)


def route(k):
    nc, ps = k.nc, k.ps
    x2 = k.x2v
    h2 = k.at(0, 12).rearrange("p (s n) -> p s n", s=3)
    h2t = k.at(12, 8).rearrange("p (s n) -> p s n", s=2)
    sq = k.at(20, 4)
    rw = k.at(24, 1)[:, 0:128].rearrange("p (k e) -> p k e", k=KD)
    lg = k.at(25, 1)[:, 0:128].rearrange("p (m e) -> p m e", m=8)
    red = k.at(26, 1)[:, 0:32]
    aff = k.at(48, 4)[0:NE, :]
    vals = k.at(52, 1)[0:NE, 0:CAP]
    idx = k.at(53, 1)[0:NE, 0:CAP].bitcast(U32)
    idf = k.at(54, 1)[0:NE, 0:CAP]
    loaded, ss, mean, rt, hh, own, tr, tev, lmm, ex, atr, own3, ftr, exd = (k.sem("r_" + n) for n in ("load", "ss", "mean", "sqrt", "h2", "own", "tr", "tev", "lmm", "exp", "atr", "own3", "ftr", "exd"))
    put = [k.sem(f"r_put{s}") for s in range(3)]
    with nc.Block() as block:
        @block.sync
        def _(sp):
            sp.dma_start(rw, k.i["router_w"].rearrange("l (k p) e -> p (l k) e", p=P)).then_inc(loaded, 16)
            for m in range(8):
                sp.wait_ge(hh, m + 1)
                sp.dma_start(k.h2[m * P:(m + 1) * P, :], h2[:, m % 3, :]).then_inc(put[m % 3], 16)
            for s in range(3):
                sp.wait_ge(put[s], 16 * len(range(s, 8, 3)))

        @block.scalar
        def _(act):
            for m in range(8):
                if m:
                    act.wait_ge(ss, m)
                nc.scalar.activation(sq, x2[:, m, :], ACT.Square, accum_out=k.rstd[:, m:m + 1]).then_inc(ss, 1)
            act.wait_ge(mean, 1)
            nc.scalar.activation(k.rstd[:, 0:8], k.rstd[:, 0:8], ACT.Sqrt).then_inc(rt, 1)
            for m in range(8):
                act.wait_ge(tr, m + 1)
                if m >= 2:
                    act.wait_ge(lmm, m - 1)
                nc.scalar.activation(h2t[:, m % 2, :], ps[:, 2 * (m % 2):2 * (m % 2) + 2, :].rearrange("p b n -> p (b n)"), ACT.Copy).then_inc(tev, 1)
            act.wait_ge(ex, 1)
            nc.scalar.activation(lg, lg, ACT.Exp).then_inc(exd, 1)

        def logits(pe, m):
            pe.wait_ge(tev, m + 1)
            for kk in range(KD):
                last = nc.tensor.matmul(ps[:, 4, m * NE:(m + 1) * NE], h2t[:, m % 2, kk * P:(kk + 1) * P], rw[:, kk, :], start=kk == 0, stop=kk == KD - 1)
            last.then_inc(lmm, 1)

        @block.tensor
        def _(pe):
            pe.wait_ge(loaded, 16)
            for m in range(8):
                pe.wait_ge(hh, m + 1)
                if m >= 2:
                    pe.wait_ge(tev, m - 1)
                for kk in range(KD):
                    last = nc.tensor.transpose(ps[:, 2 * (m % 2) + kk // 4, (kk % 4) * P:(kk % 4 + 1) * P], h2[:, m % 3, kk * P:(kk + 1) * P], k.ident)
                last.then_inc(tr, 1)
                if m:
                    logits(pe, m - 1)
            logits(pe, 7)
            pe.wait_ge(ex, 2)
            for m in range(8):
                last = nc.tensor.transpose(ps[0:NE, 5 + m // 4, (m % 4) * P:(m % 4 + 1) * P], lg[:, m, :], k.ident)
            last.then_inc(atr, 1)
            pe.wait_ge(ex, 3)
            nc.tensor.transpose(ps[:, 4, 0:NE], vals, k.ident[0:NE, 0:NE])
            nc.tensor.transpose(ps[:, 4, NE:2 * NE], idf, k.ident[0:NE, 0:NE]).then_inc(ftr, 1)

        @block.vector
        def _(dve):
            link = Links(dve, own)
            dve.wait_ge(ss, 8)
            r = k.rstd[:, 0:8]
            nc.vector.tensor_scalar(r, r, 1.0 / D, EPS, ALU.mult, ALU.add).then_inc(mean, 1)
            dve.wait_ge(rt, 1)
            link(nc.vector.reciprocal(r, r))
            for m in range(8):
                if m >= 3:
                    dve.wait_ge(put[m % 3], 16 * (m // 3))
                    dve.wait_ge(tr, m - 2)
                o = h2[:, m % 3, :]
                link(nc.vector.scalar_tensor_tensor(o, x2[:, m, :], k.rstd[:, m:m + 1], k.bc[:, k.A2, :], ALU.mult, ALU.mult))
                nc.vector.tensor_tensor(o, o, k.bc[:, k.SH2, :], ALU.add).then_inc(hh, 1)
            dve.wait_ge(lmm, 8)
            z = ps[:, 4, 0:128].rearrange("p (m e) -> p m e", m=8)
            mx, sm = red[:, 0:8], red[:, 8:16]
            link(nc.vector.tensor_reduce(mx, z, AX.X, ALU.max))
            nc.vector.tensor_tensor(lg, z, bcast(mx, [P, 8, NE]), ALU.subtract).then_inc(ex, 1)
            dve.wait_ge(exd, 1)
            link(nc.vector.tensor_reduce(sm, lg, AX.X, ALU.add))
            link(nc.vector.reciprocal(sm, sm))
            nc.vector.tensor_tensor(lg, lg, bcast(sm, [P, 8, NE]), ALU.mult).then_inc(ex, 1)
            dve.wait_ge(atr, 1)
            link(nc.vector.tensor_copy(aff, ps[0:NE, 5:7, :].rearrange("p b n -> p (b n)")))
            for i in range(CAP // 8):
                s = slice(8 * i, 8 * i + 8)
                link(nc.vector.max(vals[:, s], aff))
                nc.vector.max_index(idx[:, s], vals[:, s], aff)
                link(nc.vector.match_replace(aff, vals[:, s], aff, -1.0))
            nc.vector.tensor_copy(idf, idx).then_inc(ex, 1)
            dve.wait_ge(ftr, 1)
            nc.vector.tensor_copy(k.gate_t, ps[:, 4, 0:NE])
            link(nc.vector.tensor_copy(k.idx_t, ps[:, 4, NE:2 * NE]))


def experts(k):
    nc, ps = k.nc, k.ps
    W = 512
    widths = [(f, min(W, FF - f)) for f in range(0, FF, W)]
    NCW = len(widths)
    FT = FF // P
    NS = 6
    LOADS = 3 * NCW
    assert LOADS % NS == 0
    ring = k.at(0, 16 * NS).rearrange("p (s n) -> p s n", s=NS)
    pos = 16 * NS
    xe = k.at(pos, 4)
    xt = k.at(pos + 4, 4).rearrange("p (k t) -> p k t", k=KD)
    act_ = k.at(pos + 8, 11)
    actt = k.at(pos + 19, 11).rearrange("p (f t) -> p f t", t=P)
    ye = k.at(pos + 30, 4)
    sg = k.at(pos + 34, 4).rearrange("p (s n) -> p s n", s=2)
    got = [k.sem(f"e_ring{s}") for s in range(NS)]
    free = [k.sem(f"e_free{s}") for s in range(NS)]
    spared, idxr, gat, xtr, xev, silu, amul, atr, aev, yev, put = (k.sem("e_" + n) for n in ("spared", "idx", "gather", "xtr", "xev", "silu", "amul", "atr", "aev", "yev", "put"))
    USES = LOADS // NS

    def used(e, n):
        return e * USES + n // NS + 2

    NTR = -(-FT // 4)
    wg = k.i["ex_w_gate"].rearrange("l e (k p) f -> l e p k f", p=P)
    wu = k.i["ex_w_up"].rearrange("l e (k p) f -> l e p k f", p=P)
    wd = k.i["ex_w_down"].rearrange("l e (f p) n -> l e p f n", p=P)

    with nc.Block() as block:
        @block.sync
        def _(sp):
            with sp.Fori(0, NE) as e:
                for n in range(LOADS):
                    s = n % NS
                    sp.wait_ge(free[s], e * USES + n // NS + 1)
                    if n < 2 * NCW:
                        f0, w = widths[n // 2]
                        src = (wg, wu)[n % 2][0, bass.ds(e, 1), :, :, f0:f0 + w].rearrange("e p k f -> p (e k) f")
                        dst = ring[:, s, 0:KD * w].rearrange("p (k f) -> p k f", k=KD)
                    else:
                        c = n - 2 * NCW
                        t = min(4, FT - 4 * c)
                        src = wd[0, bass.ds(e, 1), :, 4 * c:4 * c + t, :].rearrange("e p f n -> p (e f) n")
                        dst = ring[:, s, 0:t * D].rearrange("p (f n) -> p f n", f=t)
                    sp.dma_start(dst, src).then_inc(got[s], 16)

        @block.gpsimd
        def _(pool):
            spare = k.small[0:1, 480:481]
            nc.gpsimd.memset(spare, 0.0).then_inc(spared, 1)
            pool.wait_ge(spared, 1)
            with pool.Fori(0, NE) as e:
                nc.gpsimd.tensor_copy(k.idx_now, k.idx_t[:, bass.ds(e, 1)].bitcast(U32)).then_inc(idxr, 1)
                pool.wait_ge(idxr, e + 1)
                pool.wait_ge(spared, 2 * e + 1)
                nc.gpsimd.tensor_tensor(spare, spare, spare, ALU.add).then_inc(spared, 1)
                pool.indirect_dma_start(xe, None, k.h2, bass.IndirectOffsetOnAxis(ap=k.idx_now, axis=0)).then_inc(gat, 16)
                pool.wait_ge(gat, e * 16 + 16)
                pool.wait_ge(yev, e + 2)
                pool.wait_ge(spared, 2 * e + 2)
                nc.gpsimd.tensor_tensor(spare, spare, spare, ALU.add).then_inc(spared, 1)
                pool.indirect_dma_start(k.moe, bass.IndirectOffsetOnAxis(ap=k.idx_now, axis=0), ye, None, compute_op=ALU.add).then_inc(put, 16)
                pool.wait_ge(put, e * 16 + 16)

        @block.tensor
        def _(pe):
            for s in range(NS):
                pe.sem_inc(free[s], 1)
            with pe.Fori(0, NE) as e:
                pe.wait_ge(gat, e * 16 + 16)
                for kk in range(KD):
                    last = nc.tensor.transpose(ps[:, 4 + kk // 4, (kk % 4) * P:(kk % 4 + 1) * P], xe[:, kk * P:(kk + 1) * P], k.ident)
                last.then_inc(xtr, 1)
                pe.wait_ge(xev, e + 1)
                for c, (f0, w) in enumerate(widths):
                    if c >= 2:
                        pe.wait_ge(amul, e * NCW + c - 1)
                    for g in range(2):
                        n = 2 * c + g
                        s = n % NS
                        pe.wait_ge(got[s], e * (16 * USES) + 16 * (n // NS + 1))
                        m = ring[:, s, 0:KD * w].rearrange("p (k f) -> p k f", k=KD)
                        for kk in range(KD):
                            last = nc.tensor.matmul(ps[:, 2 * (c % 2) + g, 0:w], xt[:, kk, :], m[:, kk, :], start=kk == 0, stop=kk == KD - 1)
                        last.then_inc(free[s], 1)
                for b in range(NTR):
                    t = min(4, FT - 4 * b)
                    pe.wait_ge(amul, e * NCW + min(b + 1, NCW))
                    if b >= 2:
                        pe.wait_ge(aev, e * NTR + b - 1)
                    for i in range(t):
                        f = 4 * b + i
                        last = nc.tensor.transpose(ps[:, 4 + b % 2, i * P:(i + 1) * P], act_[:, f * P:(f + 1) * P], k.ident)
                    last.then_inc(atr, 1)
                pe.wait_ge(yev, e + 1)
                for c in range(NCW):
                    t = min(4, FT - 4 * c)
                    n = 2 * NCW + c
                    s = n % NS
                    pe.wait_ge(got[s], e * (16 * USES) + 16 * (n // NS + 1))
                    pe.wait_ge(aev, e * NTR + c + 1)
                    for h in range(2):
                        for i in range(t):
                            f = 4 * c + i
                            last = nc.tensor.matmul(ps[:, 6 + h, :], actt[:, f, :], ring[:, s, i * D + h * 512:i * D + (h + 1) * 512], start=f == 0, stop=f == FT - 1)
                    last.then_inc(free[s], 1)

        @block.scalar
        def _(act):
            with act.Fori(0, NE) as e:
                act.wait_ge(xtr, e + 1)
                nc.scalar.activation(xt.rearrange("p k t -> p (k t)"), ps[:, 4:6, :].rearrange("p b n -> p (b n)"), ACT.Copy).then_inc(xev, 1)
                for c, (f0, w) in enumerate(widths):
                    act.wait_ge(free[2 * c % NS], used(e, 2 * c))
                    nc.scalar.activation(sg[:, c % 2, 0:w], ps[:, 2 * (c % 2), 0:w], ACT.Silu).then_inc(silu, 1)
                for b in range(NTR):
                    t = min(4, FT - 4 * b)
                    act.wait_ge(atr, e * NTR + b + 1)
                    nc.scalar.activation(actt[:, 4 * b:4 * b + t, :].rearrange("p f t -> p (f t)"), ps[:, 4 + b % 2, 0:t * P], ACT.Copy).then_inc(aev, 1)

        @block.vector
        def _(dve):
            dve.sem_inc(yev, 1)
            with dve.Fori(0, NE) as e:
                for c, (f0, w) in enumerate(widths):
                    dve.wait_ge(silu, e * NCW + c + 1)
                    dve.wait_ge(free[(2 * c + 1) % NS], used(e, 2 * c + 1))
                    nc.vector.tensor_tensor(act_[:, f0:f0 + w], sg[:, c % 2, 0:w], ps[:, 2 * (c % 2) + 1, 0:w], ALU.mult).then_inc(amul, 1)
                dve.wait_ge(free[(LOADS - 1) % NS], used(e, LOADS - 1))
                dve.wait_ge(idxr, e + 1)
                nc.vector.tensor_scalar(ye, ps[:, 6:8, :].rearrange("p b n -> p (b n)"), k.gate_t[:, bass.ds(e, 1)], None, ALU.mult).then_inc(yev, 1)


def finish(k):
    nc = k.nc
    x2 = k.x2v
    m_ = k.at(0, 32).rearrange("p (m n) -> p m n", m=8)
    sq = k.at(32, 4)
    loaded, add, ss, mean, rt, put, own = (k.sem("z_" + n) for n in ("load", "add", "ss", "mean", "sqrt", "put", "own"))
    outd = k.sem("z_out")
    with nc.Block() as block:
        @block.sync
        def _(sp):
            sp.dma_start(m_, k.moe.rearrange("(m p) n -> p m n", p=P)).then_inc(loaded, 16)
            for m in range(8):
                sp.wait_ge(put, m + 1)
                sp.dma_start(k.out[0, m * P:(m + 1) * P, :], m_[:, m, :]).then_inc(outd, 16)
            sp.wait_ge(outd, 128)

        @block.scalar
        def _(act):
            for m in range(8):
                act.wait_ge(add, m + 1)
                if m:
                    act.wait_ge(ss, m)
                nc.scalar.activation(sq, x2[:, m, :], ACT.Square, accum_out=k.rstd[:, m:m + 1]).then_inc(ss, 1)
            act.wait_ge(mean, 1)
            nc.scalar.activation(k.rstd[:, 0:8], k.rstd[:, 0:8], ACT.Sqrt).then_inc(rt, 1)

        @block.vector
        def _(dve):
            link = Links(dve, own)
            dve.wait_ge(loaded, 16)
            for m in range(8):
                link(nc.vector.tensor_tensor(m_[:, m, :], m_[:, m, :], k.bc[:, k.G2, :], ALU.mult))
                nc.vector.tensor_tensor(x2[:, m, :], x2[:, m, :], m_[:, m, :], ALU.add).then_inc(add, 1)
            dve.wait_ge(ss, 8)
            dve.wait_ge(add, 8)
            r = k.rstd[:, 0:8]
            nc.vector.tensor_scalar(r, r, 1.0 / D, EPS, ALU.mult, ALU.add).then_inc(mean, 1)
            dve.wait_ge(rt, 1)
            link(nc.vector.reciprocal(r, r))
            for m in range(8):
                nc.vector.scalar_tensor_tensor(m_[:, m, :], x2[:, m, :], k.rstd[:, m:m + 1], k.bc[:, k.FG, :], ALU.mult, ALU.mult).then_inc(put, 1)


def build(nc, ins, consts, out, until=99):
    with ExitStack() as ctx:
        k = Core(nc, ctx, ins, consts, out)
        k.x2v = k.at(140, 32).rearrange("p (m n) -> p m n", m=8)
        stages = [lambda: modulation(k), lambda: filters(k, 0), lambda: projection(k), lambda: long_conv(k, 0), lambda: filters(k, 1),
                  lambda: long_conv(k, 1), lambda: s5(k), lambda: glu_and_out(k), lambda: route(k), lambda: experts(k), lambda: finish(k)]
        for s in stages[:until]:
            s()
            k.end_stage()


_INS = ["x", "c", "ctx", "c_ctx", "mod_w", "mod_b", "norm1_g", "norm2_g", "w_in", "w_out", "conv_w", "conv_b",
        "hy_w1", "hy_b1", "hy_freq", "hy_w2", "hy_b2", "hy_w3", "hy_b3", "hy_bias",
        "s5_lam_re", "s5_lam_im", "s5_log_step", "s5_b_re", "s5_b_im", "s5_c_re", "s5_c_im", "s5_d",
        "s5_glu_w", "s5_glu_b", "router_w", "ex_w_gate", "ex_w_up", "ex_w_down", "final_g"]


def kernel(**inputs):
    import numpy as _np
    import concourse.bacc as _bacc
    from concourse import mybir as _mybir
    from concourse.bass_utils import run_bass_kernel_spmd as _run

    nc = _bacc.Bacc("TRN2", target_bir_lowering=False, num_devices=1)
    arrays, ins, consts = {}, {}, {}
    for name in _INS:
        a = _np.ascontiguousarray(inputs[name])
        arrays[f"in_{name}"] = a
        ins[name] = nc.dram_tensor(f"in_{name}", a.shape, _mybir.dt.from_np(a.dtype), kind="ExternalInput").ap()
    for name, a in shape_constants().items():
        arrays[f"const_{name}"] = a
        consts[name] = nc.dram_tensor(f"const_{name}", a.shape, _mybir.dt.from_np(a.dtype), kind="ExternalInput").ap()
    out = nc.dram_tensor("out", (1, SEQ, D), _mybir.dt.float32, kind="ExternalOutput").ap()
    build(nc, ins, consts, out)
    r = _run(nc, [arrays], core_ids=[0])
    return r.results[0]["out"]
```

```python
import math
from contextlib import ExitStack

import concourse.bass as bass
import numpy as np
from concourse import mybir

F32 = mybir.dt.float32
F32R = mybir.dt.float32r
I32 = mybir.dt.int32
U32 = mybir.dt.uint32
ALU = mybir.AluOpType
ACT = mybir.ActivationFunctionType
AX = mybir.AxisListType

P = 128
D = 1024
SEQ = 1024
CTX = 256
TOK = CTX + SEQ
KD = D // P
GRID = 64
HY = 512
HQ = HY // P
S5W = 512
NG, NP, NH = 32, 64, 16
PAIRS = NG // 2
T = 8
CH = TOK // T
CCH = CTX // T
XCH = SEQ // T
EPS = 1e-6
NE, FF, CAP = 16, 2816, 128
HALF = SEQ // 2
FEATS, FW = 33, 64
ROUND = 12582912.0
TURN = 6.2831845
INV_TURN = 1.0 / (2.0 * math.pi)
NEXP = 2 * (T + 1)
LAGS = (2 * T - 1) * NH

ROWS = {"c": (0, 8), "c_ctx": (8, 8), "norm1": (16, 8), "conv": (24, 36), "conv_b": (60, 12),
        "d": (72, 4), "glu_b": (76, 4)}
NROWS = 80


def shape_constants():
    f = np.arange(HALF, dtype=np.float64)
    tp = np.arange(HALF, dtype=np.float64)
    out = {}

    def tiles(m):
        return m.reshape(4, P, -1).transpose(1, 0, 2)

    def blocks(mats):
        a = np.stack([tiles(m) for m in mats], 1)
        return np.ascontiguousarray(a.reshape(P, 4, 4, 4, P).transpose(3, 0, 1, 2, 4)).astype(np.float32)

    def ang(shift):
        return [2 * np.pi * np.outer(2 * tp + par + shift, f + 0.5) / (2 * SEQ) for par in range(2)]

    even, odd = ang(0.0)
    out["dft_filter"] = blocks([np.cos(even), np.cos(odd), np.sin(even), np.sin(odd)])
    even, odd = ang(0.5)
    out["dft_signal"] = blocks([np.cos(even), np.cos(odd), np.sin(even), np.sin(odd)])
    inv = [fn(a).T / SEQ for a in (even, odd) for fn in (np.cos, np.sin)]
    out["dft_inverse"] = np.ascontiguousarray(np.stack([tiles(m) for m in inv])).astype(np.float32)

    t = np.concatenate([np.arange(0, SEQ, 2), np.arange(1, SEQ, 2)])
    tt = np.linspace(0.0, 1.0, SEQ, dtype=np.float32)[t].astype(np.float64)
    bands = (FEATS - 1) // 2
    omega = 2.0 * np.pi * t / SEQ
    fr = np.linspace(1e-4, bands - 1, bands)
    out["feats_t"] = np.concatenate([tt[None], np.cos(np.outer(fr, omega)), -np.sin(np.outer(fr, omega))]).astype(np.float32)
    deltas = np.abs(np.linspace(math.log(1e-2) / 0.3, math.log(1e-2) / 1.5, HY))
    out["decay"] = np.ascontiguousarray(np.exp(-np.outer(tt, deltas)).reshape(8, P, HY).transpose(1, 0, 2)).astype(np.float32)
    steps = np.concatenate([np.arange(T + 1), np.arange(T, -1, -1), np.arange(CH)])
    out["steps"] = np.tile(steps.astype(np.float32), (P, 1))
    out["identity"] = np.eye(P, dtype=np.float32)
    return out


class Links:

    def __init__(self, eng, sem):
        self.eng, self.sem, self.n = eng, sem, 0

    def __call__(self, ins):
        self.n += 1
        ins.then_inc(self.sem, 1)
        self.eng.wait_ge(self.sem, self.n)


def bcast(ap, shape):
    return ap.unsqueeze(len(shape) - 1).to_broadcast(shape)


class Core:

    def __init__(self, nc, ctx, ins, consts, out):
        self.nc, self.ctx, self.i, self.c, self.out = nc, ctx, ins, consts, out
        self.base = -(-nc.sbuf_base // 32) * 32
        self.arena = ctx.enter_context(nc.sbuf_tensor("arena", [P, 206 * 256], F32))
        self.ps = ctx.enter_context(nc.psum_tensor("psum", [P, 8, 512], F32))
        a = self.arena
        kb = 256

        def at(first, n, start=0):
            return a[:, int((start + first) * kb):int((start + first) * kb) + int(n * kb)]

        self.at = at
        self.greg = at(0, 32)
        self.x2t = at(32, 16).rearrange("p (q t) -> p q t", q=HQ)
        self.v = at(48, 16).rearrange("p (j c) -> p j c", j=8)
        self.x1 = at(64, 16).rearrange("p (j c) -> p j c", j=8)
        self.h_high, self.h_low = (self.over(f"h_{n}", 48 + 40 * i, 40).rearrange("p (k t) -> p k t", k=KD) for i, n in enumerate(("high", "low")))
        self.spec = at(88, 32).rearrange("p (a f c) -> p a f c", a=4, f=4)
        self.ring = at(120, 32).rearrange("p (s n) -> p s n", s=4)
        self.tmp = at(152, 24)
        self.bc = at(176, 20).rearrange("p (b n) -> p b n", b=5)
        small = at(196, 8)
        self.cols = small[:, 0:NROWS]
        self.mod_cols = small[:, 80:112].rearrange("p (j w) -> p j w", w=2)
        self.ident = small[:, 128:256]
        self.ones = small[:, 256:384]
        self.rstd = small[:, 384:400]
        self.inv_col = small[:, 400:404]
        self.scale1 = small[:, 404:420].rearrange("p (w k) -> p w k", w=2)
        self.gate_t = small[:, 420:436]
        self.idx_t = small[:, 436:452].bitcast(I32)
        self.idx_now = small[:, 452:453].bitcast(U32)
        self.silu_c = small[:, 460:476]
        self.inv_row = small[:, 512:1024]
        self.small = small
        self.extra = small[:, 1024:2048]
        s5p = at(204, 2)
        self.steps = s5p[:, 0:NEXP + CH]
        self.tau8, self.r8 = s5p[:, 192:224], s5p[:, 224:256]
        dram = lambda name, *shape: nc.dram_tensor(name, shape, F32).ap()
        self.s5_in, self.s5_out = dram("scratch_s5_in", 4, P, 2048), dram("scratch_s5_out", 4, P, 2048)
        self.s5_local = dram("scratch_s5_local", 32, PAIRS, LAGS)
        self.G1, self.A2, self.SH2, self.G2, self.FG = range(5)
        self.spec_d = dram("scratch_spec", P, 8192)
        self.z_u = nc.dram_tensor("scratch_u", (S5W, T, CH), F32).ap()
        self.z_y = nc.dram_tensor("scratch_y", (S5W, T, XCH), F32).ap()
        self.h2 = nc.dram_tensor("scratch_h2", (SEQ, D), F32).ap()
        self.x2d = nc.dram_tensor("scratch_x2", (SEQ, D), F32).ap()
        self.moe = nc.dram_tensor("scratch_moe", (SEQ, D), F32).ap()

        self.stage_sems = []

    def over(self, name, first, n, dtype=F32R):
        return self.nc.alloc_sbuf_tensor_at(name, [P, n * 256], dtype, offset=self.base + first * 1024)[:, :]

    def sem(self, name):
        self.stage_sems.append(self.nc.alloc_semaphore(name=name))
        return self.stage_sems[-1]

    def end_stage(self):
        if self.stage_sems:
            self.nc.clear_and_free_semaphores(self.stage_sems)
            self.nc.all_engine_barrier()
        self.stage_sems = []


def modulation(k):
    nc, ps = k.nc, k.ps
    NC = 2 * PAIRS
    rows = k.tmp[0:NROWS, 0:P]
    mod_rows = k.tmp[0:2, 128:128 + 2 * D]
    norm2 = k.tmp[:, 3400:3400 + D]
    bias = k.tmp[0:1, 4480:4480 + 1024].rearrange("p (b n) -> p b n", b=2)
    wbuf = k.at(120, 32).rearrange("p (s k n) -> p s k n", s=2, k=KD)
    zeros = k.at(116, 4)
    wmod = k.i["mod_w"].rearrange("l (k p) n -> p (l k) n", p=P)
    NCH = 6 * D // 512

    bd = k.at(0, 8).rearrange("p (r c w h) -> p r c w h", r=2, c=NC, w=2)
    ct = k.at(8, 4).rearrange("p (r c h) -> p r c h", r=2, c=NC)
    braw = k.at(12, 4).rearrange("p (r c h) -> p r c h", r=2, c=NC)
    craw = k.at(60, 8).rearrange("p (r d q w n) -> p r d q w n", r=2, d=2, q=4, w=2)
    bbar = k.at(20, 4).rearrange("p (r c h) -> p r c h", r=2, c=NC)
    srows = k.at(24, 1)[0:96, 0:P]
    steprow = k.at(25, 1)[64:96, 0:2]
    sc = [k.at(26 + 3 * i, 3)[:, 0:576].rearrange("p (c e) -> p c e", e=NEXP) for i in range(3)]
    sb = [k.at(35 + 2 * i, 2).rearrange("p (c h) -> p c h", c=NC) for i in range(2)]
    pre, pim = (k.at(39 + 2.25 * i, 2.25).rearrange("p (c e) -> p c e", e=NEXP) for i in range(2))
    t3, t4 = k.at(44, 4), k.at(48, 4)
    pt = k.at(52, 8)
    ep, et, ot = (k.at(60 + 16 * i, 16).rearrange("p (r d a n) -> p r d a n", r=2, d=2, a=8) for i in range(3))
    lw = k.at(108, 8)[0:32, 0:8 * LAGS].rearrange("p (a n) -> p a n", a=8)
    par = k.extra
    lt = par[:, 0:96]
    dt, xr, tau = par[:, 96:128], par[:, 128:160], par[:, 160:192]
    m2, q0, q1, w0, w1 = (par[:, 192 + 32 * i:224 + 32 * i] for i in range(5))
    cneg = par[:, 512:1024].rearrange("p (c h) -> p c h", c=NC)

    loaded, ready, turned, silu, mm, ev, tr, rows_in, own, zeroed, colsd = (
        k.sem("m_" + n) for n in ("rows", "const", "turned", "silu", "mm", "ev", "tr", "bc", "own", "zero", "cols"))
    wgot, bgot = ([k.sem(f"m_{n}{s}") for s in range(2)] for n in "wb")
    sload, sturned, aready, adone, spread, spown, otd, epd, str_, etd, lmm, lev, put_in, put_out, put_lw, ctd, cn = (
        k.sem("s_" + n) for n in ("load", "turned", "aready", "adone", "spread", "pown", "ot", "ep", "tr", "et", "lmm", "lev", "put_in", "put_out", "put_lw", "ct", "cneg"))
    NL = 3 + 1 + 4 + 8

    def table(eng, link, out, hh, cre, cim, first, sign, s0, s1):
        for d in range(2):
            cols = slice(d * PAIRS + 8 * hh, d * PAIRS + 8 * hh + 8)
            e = slice(first[d], first[d] + T)
            shape = [P, 8, T, NH]
            pr, pi = bcast(pre[:, cols, e], shape), bcast(pim[:, cols, e], shape)
            cr, ci = (x[:, cols, :].unsqueeze(2).to_broadcast(shape) for x in (cre, cim))
            o = [out[:, r, d].rearrange("p a (s h) -> p a s h", h=NH) for r in range(2)]
            m0, m1 = (x.rearrange("p (a s h) -> p a s h", a=8, h=NH) for x in (s0, s1))
            eng.tensor_tensor(o[0], cr, pr, ALU.mult)
            eng.tensor_tensor(o[1], cr, pi, ALU.mult)
            eng.tensor_tensor(m0, ci, pi, ALU.mult)
            link(eng.tensor_tensor(m1, ci, pr, ALU.mult))
            eng.tensor_tensor(o[0], o[0], m0, ALU.subtract)
            link(eng.tensor_tensor(o[1], o[1], m1, ALU.add))
            if sign < 0:
                link(eng.tensor_scalar(out[:, 1, d], out[:, 1, d], -1.0, None, ALU.mult))

    with nc.Block() as block:
        @block.sync
        def _(sp):
            def rows_of(name, ap):
                r, n = ROWS[name]
                sp.dma_start(rows[r:r + n, :], ap).then_inc(loaded, 16)
            rows_of("c", k.i["c"].rearrange("b (k p) -> (b k) p", p=P))
            rows_of("c_ctx", k.i["c_ctx"].rearrange("(k p) -> k p", p=P))
            rows_of("norm1", k.i["norm1_g"].rearrange("b (k p) -> (b k) p", p=P))
            rows_of("conv", k.i["conv_w"].rearrange("l w (k p) -> (l w k) p", p=P))
            rows_of("conv_b", k.i["conv_b"].rearrange("b (k p) -> (b k) p", p=P))
            rows_of("d", k.i["s5_d"].rearrange("b (k p) -> (b k) p", p=P))
            rows_of("glu_b", k.i["s5_glu_b"].rearrange("b (k p) -> (b k) p", p=P))
            sp.dma_start(k.ident, k.c["identity"]).then_inc(loaded, 16)
            for n in range(NCH):
                if n >= 2:
                    sp.wait_ge(mm, n - 1)
                sp.dma_start(wbuf[:, n % 2], wmod[:, :, n * 512:(n + 1) * 512]).then_inc(wgot[n % 2], 16)
                sp.dma_start(bias[:, n % 2, :], k.i["mod_b"][0:1, n * 512:(n + 1) * 512]).then_inc(bgot[n % 2], 16)

        @block.gpsimd
        def _(pool):
            nc.gpsimd.memset(k.ones, 1.0).then_inc(ready, 1)
            nc.gpsimd.memset(zeros, 0.0).then_inc(ready, 1)
            nc.gpsimd.memset(bd, 0.0).then_inc(ready, 1)
            pool.dma_start(norm2, k.i["norm2_g"].to_broadcast([P, D])).then_inc(rows_in, 16)
            pool.dma_start(k.bc[:, k.FG, :], k.i["final_g"].rearrange("(a n) -> a n", a=1).to_broadcast([P, D])).then_inc(rows_in, 16)
            pool.wait_ge(ready, 3)
            moe = k.moe.rearrange("(p r) n -> r p n", p=P)
            for r in range(SEQ // P):
                pool.dma_start(moe[r], zeros).then_inc(zeroed, 16)
            link = Links(pool, spown)
            pool.wait_ge(cn, 1)
            for hh in range(2):
                if hh:
                    pool.wait_ge(put_out, 32)
                    pool.wait_ge(lmm, 4)
                table(nc.gpsimd, link, ot, hh, ct[:, 0], ct[:, 1], (1, T + 1), -1, pt[:, 0:1024], pt[:, 1024:2048])
                nc.gpsimd.memset(pt[:, 0:1], 0.0).then_inc(otd, 1)
                for q in range(2):
                    pool.wait_ge(otd, hh + 1)
                    pool.dma_start(k.s5_out[2 * hh + q].rearrange("p (c n) -> p c n", c=4), ot[:, :, :, 4 * q:4 * q + 4, :].rearrange("p r d a n -> p (r d) (a n)")).then_inc(put_out, 16)
            pool.wait_ge(put_out, 64)
            pool.wait_ge(zeroed, 16 * SEQ // P)

        @block.tensor
        def _(pe):
            def chunk(n):
                pe.wait_ge(wgot[n % 2], 16 * (n // 2 + 1))
                pe.wait_ge(bgot[n % 2], 16 * (n // 2 + 1))
                if n >= 2:
                    pe.wait_ge(ev, n - 1)
                m = 2 if n < 4 else P
                o = ps[0:m, n % 2, :]
                for kk in range(KD):
                    lhs = k.silu_c[:, kk::KD] if n < 4 else k.silu_c[:, kk:kk + 1].to_broadcast([P, P])
                    nc.tensor.matmul(o, lhs, wbuf[:, n % 2, kk, :], start=kk == 0, stop=False)
                nc.tensor.matmul(o, k.ones[0:1, 0:m], bias[:, n % 2, :], start=False, stop=True).then_inc(mm, 1)

            def turn_states(hh):
                pe.wait_ge(epd, hh + 1)
                for i in range(8):
                    r, d, a = i // 4, (i // 2) % 2, 4 * (i % 2)
                    if i >= 4 or hh:
                        pe.wait_ge(etd, 8 * hh + i - 3)
                    for x in range(4):
                        last = nc.tensor.transpose(ps[:, 2 + i % 4, x * P:(x + 1) * P], ep[:, r, d, a + x, :], k.ident)
                    last.then_inc(str_, 1)

            def local(hh):
                pe.wait_ge(otd, hh + 1)
                pe.wait_ge(colsd, 3)
                for b in range(4):
                    if b >= 2 or hh:
                        pe.wait_ge(lev, 4 * hh + b - 1)
                    for x in range(2):
                        a = 2 * b + x
                        o = ps[0:32, 6 + b % 2, x * LAGS:(x + 1) * LAGS]
                        lhs = lambda r, d: bd[:, r, d * PAIRS + 8 * hh + a].rearrange("p w h -> p (w h)")
                        for r in range(2):
                            nc.tensor.matmul(o[:, 0:112], lhs(r, 1), ot[:, r, 1, a, NH:P], start=r == 0, stop=r == 1)
                        for i, (r, d) in enumerate(((0, 0), (1, 0), (0, 1), (1, 1))):
                            c = (ct[:, 0], cneg)[r]
                            nc.tensor.matmul(o[:, 112:128], lhs(r, d), c[:, d * PAIRS + 8 * hh + a, :], start=i == 0, stop=i == 3)
                        for r in range(2):
                            last = nc.tensor.matmul(o[:, 128:240], lhs(r, 0), ot[:, r, 0, a, 0:112], start=r == 0, stop=r == 1)
                    last.then_inc(lmm, 1)

            pe.wait_ge(loaded, 128)
            nc.tensor.transpose(ps[:, 7, 0:NROWS], rows, k.ident[0:NROWS, 0:NROWS]).then_inc(turned, 1)
            pe.wait_ge(silu, 1)
            pe.wait_ge(ready, 3)
            chunk(0)
            pe.wait_ge(sload, 16 * NL)
            pe.wait_ge(spread, 1)
            pe.wait_ge(colsd, 1)
            nc.tensor.transpose(ps[:, 7, 96:192], srows, k.ident[0:96, 0:96])
            for i in range(16):
                r, d, q = i // 8, (i // 4) % 2, i % 4
                last = nc.tensor.transpose(ps[:, 2 + i // 4, q * P:(q + 1) * P], craw[:, r, d, q].rearrange("p w n -> p (w n)"), k.ident)
            last.then_inc(sturned, 1)
            for n in range(1, 5):
                chunk(n)
            pe.wait_ge(ev, 4)
            pe.wait_ge(colsd, 2)
            for j in range(16):
                last = nc.tensor.transpose(ps[:, 7, 192 + 2 * j:194 + 2 * j], mod_rows[:, j * P:(j + 1) * P], k.ident[0:2, 0:2])
            last.then_inc(tr, 1)
            for n in range(5, 9):
                chunk(n)
            pe.wait_ge(ctd, 1)
            turn_states(0)
            for n in range(9, NCH):
                chunk(n)
            local(0)
            turn_states(1)
            local(1)

        @block.scalar
        def _(act):
            act.dma_start(srows[0:32, :], k.i["s5_lam_re"].rearrange("l d (a w) p -> (l d a) (w p)", w=2)).then_inc(sload, 16)
            act.dma_start(srows[32:64, :], k.i["s5_lam_im"].rearrange("l d (a w) p -> (l d a) (w p)", w=2)).then_inc(sload, 16)
            act.dma_start(steprow, k.i["s5_log_step"].rearrange("l d (a w) -> (l d a) w", w=2)).then_inc(sload, 16)
            act.dma_start(k.steps, k.c["steps"]).then_inc(sload, 16)
            for r, (nb, ncc) in enumerate((("s5_b_re", "s5_c_re"), ("s5_b_im", "s5_c_im"))):
                for d in range(2):
                    for w in range(2):
                        act.dma_start(craw[:, r, d, :, w, :], k.i[ncc][0, d].rearrange("(q g) h p -> (g h) q p", g=8)).then_inc(sload, 16)
                    act.dma_start(braw[:, r, d * PAIRS:(d + 1) * PAIRS, :], k.i[nb][0, d].rearrange("(a w) p h -> (w p) a h", w=2)).then_inc(sload, 16)
            act.wait_ge(turned, 1)
            nc.scalar.activation(k.silu_c, ps[:, 7, 0:16], ACT.Silu).then_inc(silu, 1)

            def evacuate(n):
                act.wait_ge(mm, n + 1)
                if n < 4:
                    o, p = mod_rows[:, n * 512:(n + 1) * 512], slice(0, 2)
                else:
                    which, h = divmod(n - 4, 2)
                    o, p = k.bc[:, [k.G1, k.SH2, k.A2, k.G2][which], h * 512:(h + 1) * 512], slice(0, P)
                nc.scalar.activation(o, ps[p, n % 2, :], ACT.Copy).then_inc(ev, 1)

            evacuate(0)
            act.wait_ge(aready, 1)
            nc.scalar.activation(dt, lt[:, 64:96], ACT.Exp).then_inc(adone, 1)
            evacuate(1)
            act.wait_ge(aready, 2)
            nc.scalar.activation(sc[0], sc[0], ACT.Exp).then_inc(adone, 1)
            evacuate(2)
            act.wait_ge(aready, 3)
            nc.scalar.activation(sc[1], sc[1], ACT.Sin, scale=TURN)
            nc.scalar.activation(sc[2], sc[2], ACT.Sin, scale=TURN).then_inc(adone, 1)
            for n in range(3, NCH):
                evacuate(n)
            for hh in range(2):
                act.wait_ge(etd, 8 * hh + 8)
                for q in range(2):
                    act.dma_start(k.s5_in[2 * hh + q].rearrange("p (c n) -> p c n", c=4), et[:, :, :, 4 * q:4 * q + 4, :].rearrange("p r d a n -> p (r d) (a n)")).then_inc(put_in, 16)
                act.wait_ge(lev, 4 * hh + 4)
                act.dma_start(k.s5_local[:, 8 * hh:8 * hh + 8, :], lw).then_inc(put_lw, 16)
            act.wait_ge(put_in, 64)
            act.wait_ge(put_lw, 32)

        @block.vector
        def _(dve):
            link = Links(dve, own)
            tt, ts = nc.vector.tensor_tensor, nc.vector.tensor_scalar
            dve.wait_ge(turned, 1)
            dve.wait_ge(silu, 1)
            nc.vector.tensor_copy(k.cols, ps[:, 7, 0:NROWS]).then_inc(colsd, 1)
            dve.wait_ge(sload, 16 * NL)
            nc.vector.tensor_copy(srows[64:96, :].rearrange("p (w n) -> p w n", w=2), bcast(steprow, [32, 2, NP])).then_inc(spread, 1)
            dve.wait_ge(sturned, 1)
            link(nc.vector.tensor_copy(lt, ps[:, 7, 96:192]))
            nc.vector.tensor_copy(xr, lt[:, 64:96]).then_inc(colsd, 1)
            nc.vector.tensor_copy(q0, lt[:, 64:96]).then_inc(aready, 1)
            for w in range(2):
                p = slice(NP * w, NP * w + NP)
                last = nc.vector.tensor_copy(ct[p].rearrange("p r (d a) h -> p (r d) a h", d=2), ps[p, 2:6, :].rearrange("p b (a w h) -> p w b a h", w=2, h=NH)[:, w])
            last.then_inc(ctd, 1)
            dve.wait_ge(ctd, 1)
            ts(cneg, ct[:, 1], -1.0, None, ALU.mult)
            dve.wait_ge(adone, 1)
            link(tt(xr, lt[:, 0:32], dt, ALU.mult))
            link(nc.vector.scalar_tensor_tensor(tau, lt[:, 32:64], INV_TURN, dt, ALU.mult, ALU.mult))
            e = k.steps[:, 0:NEXP].unsqueeze(1).to_broadcast([P, NC, NEXP])
            tt(sc[0], bcast(xr, [P, NC, NEXP]), e, ALU.mult).then_inc(aready, 1)
            link(tt(sc[1], bcast(tau, [P, NC, NEXP]), e, ALU.mult))
            link(ts(sc[2], sc[1], 0.25, None, ALU.add))
            for s in (sc[1], sc[2]):
                link(ts(pre, s, ROUND, ROUND, ALU.add, ALU.subtract))
                link(tt(s, s, pre, ALU.subtract))
            ts(w0, tau, float(T), None, ALU.mult).then_inc(aready, 1)
            dve.wait_ge(aready, 3)
            link(ts(w1, w0, ROUND, ROUND, ALU.add, ALU.subtract))
            tt(k.tau8, w0, w1, ALU.subtract)
            dve.wait_ge(adone, 3)
            tt(pre, sc[0], sc[2], ALU.mult)
            link(tt(pim, sc[0], sc[1], ALU.mult))
            nc.vector.tensor_copy(k.r8, sc[0][:, :, T]).then_inc(cn, 1)
            lr, li = lt[:, 0:32], lt[:, 32:64]
            link(ts(w0, pre[:, :, 1], -1.0, None, ALU.add))
            b1 = pim[:, :, 1]
            link(tt(q0, w0, lr, ALU.mult))
            link(tt(w1, b1, li, ALU.mult))
            link(tt(q0, q0, w1, ALU.add))
            link(tt(q1, b1, lr, ALU.mult))
            link(tt(w1, w0, li, ALU.mult))
            link(tt(q1, q1, w1, ALU.subtract))
            link(tt(m2, lr, lr, ALU.mult))
            link(tt(w1, li, li, ALU.mult))
            link(tt(m2, m2, w1, ALU.add))
            link(nc.vector.reciprocal(m2, m2))
            tt(q0, q0, m2, ALU.mult)
            link(tt(q1, q1, m2, ALU.mult))
            Q0, Q1 = bcast(q0, [P, NC, NH]), bcast(q1, [P, NC, NH])
            tt(bbar[:, 0], braw[:, 0], Q0, ALU.mult)
            tt(bbar[:, 1], braw[:, 0], Q1, ALU.mult)
            tt(sb[0], braw[:, 1], Q1, ALU.mult)
            link(tt(sb[1], braw[:, 1], Q0, ALU.mult))
            tt(bbar[:, 0], bbar[:, 0], sb[0], ALU.subtract)
            link(tt(bbar[:, 1], bbar[:, 1], sb[1], ALU.add))
            dve.wait_ge(ready, 3)
            for w in range(2):
                p = slice(NP * w, NP * w + NP)
                link(nc.vector.tensor_copy(bd[p, :, :, w, :], bbar[p]))
            dve.wait_ge(tr, 1)
            nc.vector.tensor_copy(k.mod_cols, ps[:, 7, 192:224].rearrange("p (j w) -> p j w", w=2)).then_inc(colsd, 1)
            dve.wait_ge(colsd, 3)
            r = ROWS["norm1"][0]
            for w in range(2):
                nc.vector.scalar_tensor_tensor(k.scale1[:, w, :], k.mod_cols[:, 8:16, w], 1.0, k.cols[:, r:r + 8], ALU.add, ALU.mult)
            for hh in range(2):
                table(nc.vector, link, ep, hh, bbar[:, 0], bbar[:, 1], (T + 2, 0), 1, t3, t4)
                nc.vector.tensor_copy(t3[:, 0:1], t4[:, 0:1]).then_inc(epd, 1)
                if hh:
                    dve.wait_ge(put_in, 32)
                for i in range(8):
                    dve.wait_ge(str_, 8 * hh + i + 1)
                    r, d, a = i // 4, (i // 2) % 2, 4 * (i % 2)
                    nc.vector.tensor_copy(et[:, r, d, a:a + 4, :], ps[:, 2 + i % 4, :].rearrange("p (a n) -> p a n", a=4)).then_inc(etd, 1)
                if hh:
                    dve.wait_ge(put_lw, 16)
                for b in range(4):
                    dve.wait_ge(lmm, 4 * hh + b + 1)
                    nc.vector.tensor_copy(lw[:, 2 * b:2 * b + 2, :], ps[0:32, 6 + b % 2, 0:2 * LAGS].rearrange("p (a n) -> p a n", a=2)).then_inc(lev, 1)
            dve.wait_ge(ev, NCH)
            dve.wait_ge(rows_in, 32)
            link(nc.vector.scalar_tensor_tensor(k.bc[:, k.A2, :], k.bc[:, k.A2, :], 1.0, norm2, ALU.add, ALU.mult))


def projection(k):
    nc, ps = k.nc, k.ps
    NT = TOK // P
    xin = k.at(0, 12).rearrange("p (s n) -> p s n", s=3)
    xn = k.at(12, 8).rearrange("p (s n) -> p s n", s=2)
    sq = k.at(20, 4)
    got, ss, own_v, own_s, norm, tr, ev, tdone = k.sem("p_x"), k.sem("p_ss"), k.sem("p_dve"), k.sem("p_act"), k.sem("p_norm"), k.sem("p_tr"), k.sem("p_ev"), k.sem("p_sqrt")
    h = k.over("p_h", 24, 8, F32).rearrange("p (s k t) -> p s k t", s=2, k=KD)
    spilled, hhi, hlo, inv = k.sem("p_spilled"), k.sem("p_hhi"), k.sem("p_hlo"), k.sem("p_inv")
    spec = k.spec.rearrange("p a f c -> p (a f c)")
    got3 = [k.sem(f"p_x{s}") for s in range(3)]

    w_in = k.i["w_in"].rearrange("l (k p) n -> p (l k) n", p=P)
    NW, NWH = 3, 3
    wraw = [k.over(f"p_wraw{s}", 128 + 8 * s, 8, F32).rearrange("p (k n) -> p k n", k=KD) for s in range(NW)]
    wlow = [k.over(f"p_wlow{s}", 128 + 8 * s, 8).rearrange("p (k n) -> p k n", k=KD) for s in range(NW)]
    whigh = [k.over(f"p_whigh{s}", 152 + 4 * s, 4).rearrange("p (k n) -> p k n", k=KD) for s in range(NWH)]
    whi, wlo = k.sem("p_whi"), k.sem("p_wlo")
    wgot = [k.sem(f"p_w{s}") for s in range(NW)]

    def load_weights(sp, g):
        sp.dma_start(wraw[g % NW], w_in[:, :, g * 256:(g + 1) * 256]).then_inc(wgot[g % NW], 16)

    with nc.Block() as block:
        @block.sync
        def _(sp):
            for n in range(NT):
                if n >= 3:
                    sp.wait_ge(norm, n - 2)
                src = k.i["ctx"][0, n * P:(n + 1) * P, :] if n < 2 else k.i["x"][0, (n - 2) * P:(n - 1) * P, :]
                sp.dma_start(xin[:, n % 3, :], src).then_inc(got3[n % 3], 16)
                if n == 2:
                    sp.dma_start(k.spec_d, spec).then_inc(spilled, 16)
            for g in range(NW):
                load_weights(sp, g)

        @block.scalar
        def _(act):
            def high_tile(n):
                act.wait_ge(ev, n + 1)
                nc.scalar.activation(k.h_high[:, :, n * P:(n + 1) * P], h[:, n % 2], ACT.Copy).then_inc(hhi, 1)

            for n in range(NT):
                act.wait_ge(got3[n % 3], 16 * (n // 3 + 1))
                if n:
                    act.wait_ge(ss, n)
                nc.scalar.activation(sq, xin[:, n % 3, :], ACT.Square, accum_out=k.rstd[:, n:n + 1]).then_inc(ss, 1)
                act.wait_ge(own_v, 1 + n)
                nc.scalar.activation(k.rstd[:, n:n + 1], k.rstd[:, n:n + 1], ACT.Sqrt).then_inc(tdone, 1)
                act.wait_ge(inv, n + 1)
                if n >= 2:
                    act.wait_ge(tr, n - 1)
                nc.scalar.activation(xn[:, n % 2, :], xin[:, n % 3, :], ACT.Copy, scale=k.rstd[:, n:n + 1]).then_inc(norm, 1)
                if n:
                    high_tile(n - 1)
            high_tile(NT - 1)

        def evacuate(dve, n):
            dve.wait_ge(tr, n + 1)
            if n >= 2:
                dve.wait_ge(hhi, n - 1)
                dve.wait_ge(hlo, n - 1)
            w = 1 if n < 2 else 0
            for kk in range(KD):
                last = nc.vector.tensor_scalar(h[:, n % 2, kk], ps[:, 2 * (n % 2) + kk // 4, (kk % 4) * P:(kk % 4 + 1) * P],
                                               k.scale1[:, w, kk:kk + 1], k.mod_cols[:, kk, w:w + 1], ALU.mult, ALU.add)
            last.then_inc(ev, 1)

        @block.gpsimd
        def _(pool):
            pool.wait_ge(spilled, 16)
            for n in range(NT):
                t = slice(n * P, (n + 1) * P)
                pool.wait_ge(hhi, n + 1)
                nc.gpsimd.tensor_tensor(k.h_low[:, :, t], h[:, n % 2], k.h_high[:, :, t].bitcast(F32), ALU.subtract).then_inc(hlo, 1)

        @block.vector
        def _(dve):
            link = Links(dve, own_v)
            for n in range(NT):
                dve.wait_ge(ss, n + 1)
                r = k.rstd[:, n:n + 1]
                link(nc.vector.tensor_scalar(r, r, 1.0 / D, EPS, ALU.mult, ALU.add))
                dve.wait_ge(tdone, n + 1)
                nc.vector.reciprocal(r, r).then_inc(inv, 1)
                if n:
                    evacuate(dve, n - 1)
            evacuate(dve, NT - 1)

        @block.tensor
        def _(pe):
            for n in range(NT):
                pe.wait_ge(norm, n + 1)
                if n >= 2:
                    pe.wait_ge(ev, n - 1)
                for kk in range(KD):
                    last = nc.tensor.transpose(ps[:, 2 * (n % 2) + kk // 4, (kk % 4) * P:(kk % 4 + 1) * P], xn[:, n % 2, kk * P:(kk + 1) * P], k.ident)
                last.then_inc(tr, 1)

    z_t = k.greg.rearrange("p (q t) -> p q t", q=2 * HQ)
    ubuf = k.at(164, 12)[:, 0:2 * TOK].rearrange("p (s n) -> p s n", s=2)
    mm, mid, conv, uout, own2 = k.sem("p_mm"), k.sem("p_mid"), k.sem("p_conv"), [k.sem(f"p_uout{s}") for s in range(2)], k.sem("p_own2")
    NCT = 16

    def half(slots, c):
        return slots[(c // 2) % NW][:, :, (c % 2) * P:(c % 2 + 1) * P]

    with nc.Block() as block:
        @block.sync
        def _(sp):
            for g in range(NW, NCT // 2):
                sp.wait_ge(mm, 2 * (g - NW) + 2)
                load_weights(sp, g)
            for q in range(HQ):
                sp.wait_ge(conv, 12 + q + 1)
                sp.dma_start(k.z_u[q * P:(q + 1) * P].rearrange("p s k -> p (s k)"), ubuf[:, q % 2, :]).then_inc(uout[q % 2], 16)
            sp.wait_ge(uout[0], 32)
            sp.wait_ge(uout[1], 32)

        @block.tensor
        def _(pe):
            for c in range(NCT):
                pe.wait_ge(wlo, c + 1)
                if c >= 2:
                    pe.wait_ge(conv, c - 1)
                b0 = 4 * (c % 2)
                spans = [(CTX, 512), (CTX + 512, 512)] + ([(0, CTX)] if c >= 12 else [])
                for b, (t0, n) in enumerate(spans):
                    for kk in range(KD):
                        o, t = ps[:, b0 + b, 0:n], slice(t0, t0 + n)
                        nc.tensor.matmul(o, whigh[c % NWH][:, kk], k.h_high[:, kk, t], start=kk == 0, stop=False)
                        nc.tensor.matmul(o, whigh[c % NWH][:, kk], k.h_low[:, kk, t], start=False, stop=False)
                        last = nc.tensor.matmul(o, half(wlow, c)[:, kk], k.h_high[:, kk, t], start=False, stop=kk == KD - 1)
                last.then_inc(mm, 1)

        def out_of(c):
            if c < 8:
                return z_t[:, c, :]
            return k.x2t[:, c - 8, :]

        @block.scalar
        def _(act):
            def high_part(c):
                act.wait_ge(wgot[(c // 2) % NW], 16 * (c // 2 // NW + 1))
                if c >= NWH:
                    act.wait_ge(mm, c - NWH + 1)
                nc.scalar.activation(whigh[c % NWH], half(wraw, c), ACT.Copy).then_inc(whi, 1)

            high_part(0)
            high_part(1)
            for c in range(NCT):
                if c + 2 < NCT:
                    high_part(c + 2)
                if c >= 12:
                    continue
                act.wait_ge(mm, c + 1)
                r0, rb = ROWS["conv"][0], ROWS["conv_b"][0]
                z = ps[:, 4 * (c % 2):4 * (c % 2) + 2, :].rearrange("p b n -> p (b n)")
                nc.scalar.activation(out_of(c), z, ACT.Identity, bias=k.cols[:, rb + c:rb + c + 1], scale=k.cols[:, r0 + 12 + c:r0 + 13 + c]).then_inc(mid, 1)

        @block.vector
        def _(dve):
            link = Links(dve, own2)

            def low_part(c):
                if c < NCT:
                    dve.wait_ge(whi, c + 1)
                    nc.vector.tensor_tensor(half(wlow, c), half(wraw, c), whigh[c % NWH].bitcast(F32), ALU.subtract).then_inc(wlo, 1)

            low_part(0)
            low_part(1)
            for c in range(12):
                low_part(c + 2)
                dve.wait_ge(mid, c + 1)
                z = ps[:, 4 * (c % 2):4 * (c % 2) + 2, :].rearrange("p b (r t) -> p (b r) t", t=GRID)
                o = out_of(c).rearrange("p (r t) -> p r t", t=GRID)
                r0 = ROWS["conv"][0]
                link(nc.vector.scalar_tensor_tensor(o[:, :, 1:GRID], z[:, :, 0:GRID - 1], k.cols[:, r0 + c:r0 + c + 1], o[:, :, 1:GRID], ALU.mult, ALU.add))
                nc.vector.scalar_tensor_tensor(o[:, :, 0:GRID - 1], z[:, :, 1:GRID], k.cols[:, r0 + 24 + c:r0 + 25 + c], o[:, :, 0:GRID - 1], ALU.mult, ALU.add).then_inc(conv, 1)
            for q in range(HQ):
                c = 12 + q
                low_part(c + 2)
                dve.wait_ge(mm, c + 1)
                if q >= 2:
                    dve.wait_ge(uout[q % 2], 16)
                o = ubuf[:, q % 2, :].rearrange("p (s k) -> p s k", s=T)
                b0 = 4 * (c % 2)
                nc.vector.tensor_copy(o[:, :, 0:CCH], ps[:, b0 + 2, 0:CTX].rearrange("p (k s) -> p s k", s=T))
                z = ps[:, b0:b0 + 2, :].rearrange("p b (k s) -> p s (b k)", s=T)
                nc.vector.tensor_copy(o[:, :, CCH:CH], z).then_inc(conv, 1)

    tr, ev, back = k.sem("v_tr"), k.sem("v_ev"), k.sem("v_spec")
    with nc.Block() as block:
        @block.sync
        def _(sp):
            sp.dma_start(spec, k.spec_d).then_inc(back, 16)
            sp.wait_ge(back, 16)

        @block.tensor
        def _(pe):
            for n in range(16):
                which, j = n % 2, n // 2
                if n >= 4:
                    pe.wait_ge(ev, n - 3)
                for q in range(HQ):
                    src = z_t[:, which * HQ + q, :].rearrange("p (t r) -> p r t", r=2)[:, j // 4, (j % 4) * P:(j % 4 + 1) * P]
                    last = nc.tensor.transpose(ps[:, n % 4, q * P:(q + 1) * P], src, k.ident)
                last.then_inc(tr, 1)

        @block.vector
        def _(dve):
            for n in range(16):
                which, j = n % 2, n // 2
                dve.wait_ge(tr, n + 1)
                if which:
                    nc.vector.tensor_tensor(k.x1[:, j, :], ps[:, n % 4, :], k.inv_row, ALU.mult).then_inc(ev, 1)
                else:
                    nc.vector.tensor_copy(k.v[:, j, :], ps[:, n % 4, :]).then_inc(ev, 1)


def filters(k, order):
    nc, ps = k.nc, k.ps
    tag = f"f{order}_"
    sd = k.greg.rearrange("p (w j c) -> p w j c", w=2, j=8)
    w1 = k.tmp[0:FEATS, 0:FW]
    w2 = k.tmp[0:FW, 64:128]
    vec = k.tmp[0:FW, 128:136]
    feats = k.at(120, 4)[0:FEATS, :]
    w3 = k.at(124, 8)[0:FW, 0:2 * HY]
    b3 = k.at(128, 4)[0:1, :]
    decay = k.at(132, 16).rearrange("p (j c) -> p j c", j=8)
    hid = [k.tmp[0:FW, 256 + i * SEQ:256 + (i + 1) * SEQ] for i in range(3)]
    fb = k.tmp[:, 3584:3584 + 4 * HY].rearrange("p (w c) -> p w c", w=4)
    hyb = k.extra[0:1, 0:HY]
    ab = k.at(64, 8).rearrange("p (b w c) -> p b w c", b=2, w=2)
    absd = k.sem(tag + "abs")
    acc = k.extra[:, HY:2 * HY]
    loaded, mm, sv, own, kf, pss, sine = k.sem(tag + "load"), k.sem(tag + "mm"), k.sem(tag + "scale"), k.sem(tag + "own"), k.sem(tag + "k"), k.sem(tag + "norm"), k.sem(tag + "sine")
    hready = k.sem(tag + "h")

    with nc.Block() as block:
        @block.sync
        def _(sp):
            n = 0
            for ap, src in ((w1, k.i["hy_w1"][0]), (w2, k.i["hy_w2"][0]), (feats, k.c["feats_t"]),
                            (vec[:, 0:1], k.i["hy_b1"].rearrange("l n -> n l")), (vec[:, 1:2], k.i["hy_b2"].rearrange("l n -> n l")),
                            (vec[:, 2:3], k.i["hy_freq"][0, 0:1].rearrange("l n -> n l")), (vec[:, 3:4], k.i["hy_freq"][0, 1:2].rearrange("l n -> n l")),
                            (w3, k.i["hy_w3"][0, :, order * 2 * HY:(order + 1) * 2 * HY]), (b3, k.i["hy_b3"][:, order * 2 * HY:(order + 1) * 2 * HY]),
                            (decay, k.c["decay"]), (hyb, k.i["hy_bias"][0, order:order + 1, :])):
                sp.dma_start(ap, src).then_inc(loaded, 16)
            sp.wait_ge(loaded, 11 * 16)

        @block.tensor
        def _(pe):
            pe.wait_ge(loaded, 11 * 16)
            for layer in range(2):
                for h in range(2):
                    if layer:
                        pe.wait_ge(sine, 1)
                        nc.tensor.matmul(ps[0:FW, 2 + h, :], w2, hid[2][:, h * 512:(h + 1) * 512], start=True, stop=True).then_inc(mm, 1)
                    else:
                        nc.tensor.matmul(ps[0:FW, h, :], w1, feats[:, h * 512:(h + 1) * 512], start=True, stop=True).then_inc(mm, 1)
            pe.wait_ge(sine, 2)
            for j in range(8):
                if j >= 2:
                    pe.wait_ge(kf, j - 1)
                for d in range(2):
                    o = ps[:, 4 + 2 * (j % 2) + d, :]
                    nc.tensor.matmul(o, hid[2][:, j * P:(j + 1) * P], w3[:, d * HY:(d + 1) * HY], start=True, stop=False)
                    last = nc.tensor.matmul(o, k.ones[0:1, :], b3[:, d * HY:(d + 1) * HY], start=False, stop=True)
                last.then_inc(mm, 1)
            pe.wait_ge(pss, 15)
            nc.tensor.matmul(ps[:, 0, :], k.ones, acc, start=True, stop=True)
            for q in range(HQ):
                last = nc.tensor.matmul(ps[:, 1, q:q + 1], acc[:, q * P:(q + 1) * P], k.ones[:, 0:1], start=True, stop=True)
            last.then_inc(mm, 1)

        @block.gpsimd
        def _(pool):
            for j in range(8):
                pool.wait_ge(absd, j + 1)
                if j == 0:
                    nc.gpsimd.tensor_tensor(acc, ab[:, 0, 0, :], ab[:, 0, 1, :], ALU.add).then_inc(pss, 1)
                    pool.wait_ge(pss, 1)
                else:
                    for w in range(2):
                        nc.gpsimd.tensor_tensor(acc, acc, ab[:, j % 2, w, :], ALU.add).then_inc(pss, 1)
                        pool.wait_ge(pss, 2 * j + w)

        @block.scalar
        def _(act):
            for layer in range(2):
                act.wait_ge(hready, layer + 1)
                nc.scalar.activation(hid[2], hid[1], ACT.Sin, scale=TURN).then_inc(sine, 1)
            for j in range(8):
                act.wait_ge(kf, j + 1)
                if j >= 2:
                    act.wait_ge(pss, 2 * j - 3)
                nc.scalar.activation(ab[:, j % 2], fb[:, 2 * (j % 2):2 * (j % 2) + 2, :], ACT.Abs).then_inc(absd, 1)

        @block.vector
        def _(dve):
            link = Links(dve, own)
            dve.wait_ge(loaded, 11 * 16)
            link(nc.vector.tensor_scalar(vec[:, 4:6], vec[:, 2:4], INV_TURN, None, ALU.mult))
            for layer in range(2):
                dve.wait_ge(mm, 2 * layer + 2)
                z = ps[0:FW, 2 * layer:2 * layer + 2, :].rearrange("p b n -> p (b n)")
                link(nc.vector.tensor_scalar(hid[0], z, vec[:, layer:layer + 1], vec[:, 4 + layer:5 + layer], ALU.add, ALU.mult))
                link(nc.vector.tensor_scalar(hid[1], hid[0], ROUND, ROUND, ALU.add, ALU.subtract))
                nc.vector.tensor_tensor(hid[1], hid[0], hid[1], ALU.subtract).then_inc(hready, 1)
            for j in range(8):
                dve.wait_ge(mm, 4 + j + 1)
                b = 4 + 2 * (j % 2)
                s, d = sd[:, 0, j, :], sd[:, 1, j, :]
                fw, bw = fb[:, 2 * (j % 2), :], fb[:, 2 * (j % 2) + 1, :]
                if j >= 2:
                    dve.wait_ge(absd, j - 1)
                nc.vector.tensor_tensor(fw, ps[:, b, :], decay[:, j, :], ALU.mult)
                link(nc.vector.tensor_tensor(bw, ps[:, b + 1, :], decay[:, j, :], ALU.mult))
                if j == 0:
                    link(nc.vector.memset(fb[0:1, 1, :], 0.0))
                nc.vector.tensor_tensor(s, fw, bw, ALU.add)
                nc.vector.tensor_tensor(d, bw, fw, ALU.subtract).then_inc(kf, 1)
            dve.wait_ge(mm, 13)
            dve.wait_ge(kf, 8)
            dve.wait_ge(absd, 8)
            link(nc.vector.tensor_tensor(fb[0:1, 2, :], hyb, ps[0:1, 0, :], ALU.mult))
            nc.vector.tensor_tensor(sd[0:1, 0, 0, :], sd[0:1, 0, 0, :], fb[0:1, 2, :], ALU.add)
            nc.vector.reciprocal(k.inv_row, ps[:, 0, :])
            nc.vector.reciprocal(k.inv_col, ps[:, 1, 0:HQ])

    ring = [k.sem(tag + f"ring{s}") for s in range(4)]
    mm2, cp, own2, done = k.sem(tag + "mm2"), k.sem(tag + "cp"), k.sem(tag + "own2"), k.sem(tag + "done")
    half = k.tmp[:, 0:4 * HY].rearrange("p (b w c) -> p b w c", b=2, w=2)
    with nc.Block() as block:
        @block.sync
        def _(sp):
            for f in range(4):
                sp.dma_start(k.ring[:, f, :], k.c["dft_filter"][f].rearrange("p m k n -> p (m k n)")).then_inc(ring[f], 16)

        @block.tensor
        def _(pe):
            for f in range(4):
                pe.wait_ge(ring[f], 16)
                if f >= 2:
                    pe.wait_ge(done, f - 1)
                m = k.ring[:, f, :].rearrange("p (m k n) -> p m k n", m=4, k=4)
                for mat in range(4):
                    for kk in range(4):
                        last = nc.tensor.matmul(ps[:, 4 * (f % 2) + mat, :], m[:, mat, kk, :], sd[:, mat // 2, 4 * (mat % 2) + kk, :], start=kk == 0, stop=kk == 3)
                last.then_inc(mm2, 1)

        @block.scalar
        def _(act):
            for f in range(4):
                act.wait_ge(mm2, f + 1)
                if f >= 2:
                    act.wait_ge(done, f - 1)
                nc.scalar.activation(half[:, f % 2, 0, :], ps[:, 4 * (f % 2) + 1, :], ACT.Copy)
                nc.scalar.activation(half[:, f % 2, 1, :], ps[:, 4 * (f % 2) + 3, :], ACT.Copy).then_inc(cp, 1)

        @block.vector
        def _(dve):
            for f in range(4):
                dve.wait_ge(cp, f + 1)
                b = 4 * (f % 2)
                co, so = half[:, f % 2, 0, :], half[:, f % 2, 1, :]
                nc.vector.tensor_tensor(k.spec[:, 0, f, :], ps[:, b, :], co, ALU.add)
                nc.vector.tensor_tensor(k.spec[:, 1, f, :], ps[:, b + 2, :], so, ALU.add)
                nc.vector.tensor_tensor(k.spec[:, 2, f, :], ps[:, b, :], co, ALU.subtract)
                nc.vector.tensor_tensor(k.spec[:, 3, f, :], so, ps[:, b + 2, :], ALU.subtract).then_inc(done, 1)


def long_conv(k, order):
    nc, ps = k.nc, k.ps
    tag = f"l{order}_"
    g = k.greg.rearrange("p (a f c) -> p a f c", a=4, f=4)
    ring = [k.sem(tag + f"ring{s}") for s in range(4)]
    half = k.at(152, 8).rearrange("p (b w c) -> p b w c", b=2, w=2)
    u = k.at(160, 16).rearrange("p (w c) -> p w c", w=8)
    mm, cp, own, done, inv, fin = k.sem(tag + "mm"), k.sem(tag + "cp"), k.sem(tag + "own"), k.sem(tag + "done"), k.sem(tag + "inv"), k.sem(tag + "fin")
    with nc.Block() as block:
        @block.sync
        def _(sp):
            for f in range(4):
                sp.dma_start(k.ring[:, f, :], k.c["dft_signal"][f].rearrange("p m k n -> p (m k n)")).then_inc(ring[f], 16)
            for i in range(4):
                sp.wait_ge(mm, i + 1)
                sp.dma_start(k.ring[:, i, :], k.c["dft_inverse"][i].rearrange("p k n -> p (k n)")).then_inc(ring[i], 16)

        @block.tensor
        def _(pe):
            for f in range(4):
                pe.wait_ge(ring[f], 16)
                if f >= 2:
                    pe.wait_ge(done, f - 1)
                m = k.ring[:, f, :].rearrange("p (m k n) -> p m k n", m=4, k=4)
                for mat in range(4):
                    for kk in range(4):
                        last = nc.tensor.matmul(ps[:, 4 * (f % 2) + mat, :], m[:, mat, kk, :], k.v[:, 4 * (mat % 2) + kk, :], start=kk == 0, stop=kk == 3)
                last.then_inc(mm, 1)
            pe.wait_ge(done, 4)
            for n in range(8):
                par, tile = divmod(n, 4)
                if n % 4 == 0:
                    pe.wait_ge(ring[2 * par], 32)
                    pe.wait_ge(ring[2 * par + 1], 32)
                if n >= 4:
                    pe.wait_ge(fin, n - 3)
                for cs in range(2):
                    m = k.ring[:, 2 * par + cs, :].rearrange("p (k n) -> p k n", k=4)
                    for kk in range(4):
                        a, b = m[:, kk, :], g[:, 2 * par + cs, kk, :]
                        a, b = (a[:, tile * P:(tile + 1) * P], b) if order == 0 else (b[:, tile * P:(tile + 1) * P], a)
                        last = nc.tensor.matmul(ps[:, n % 4, :], a, b, start=cs + kk == 0, stop=cs == 1 and kk == 3)
                last.then_inc(inv, 1)

        @block.scalar
        def _(act):
            for f in range(4):
                act.wait_ge(mm, f + 1)
                if f >= 2:
                    act.wait_ge(done, f - 1)
                nc.scalar.activation(half[:, f % 2, 0, :], ps[:, 4 * (f % 2) + 1, :], ACT.Copy)
                nc.scalar.activation(half[:, f % 2, 1, :], ps[:, 4 * (f % 2) + 3, :], ACT.Copy).then_inc(cp, 1)

        @block.vector
        def _(dve):
            link = Links(dve, own)
            tt = nc.vector.tensor_tensor
            for f in range(4):
                dve.wait_ge(cp, f + 1)
                b = 4 * (f % 2)
                co, so = half[:, f % 2, 0, :], half[:, f % 2, 1, :]
                re, um, reb, umb = (u[:, i, :] for i in range(4))
                tt(re, ps[:, b, :], co, ALU.add)
                tt(umb, ps[:, b, :], co, ALU.subtract)
                tt(um, ps[:, b + 2, :], so, ALU.add)
                link(tt(reb, ps[:, b + 2, :], so, ALU.subtract))
                for bar, (a, m) in enumerate(((re, um), (reb, umb))):
                    kre, kim = k.spec[:, 2 * bar, f, :], k.spec[:, 2 * bar + 1, f, :]
                    t0, t1, t2, t3 = (u[:, 4 + i, :] for i in range(4))
                    tt(t0, a, kre, ALU.mult)
                    tt(t1, m, kim, ALU.mult)
                    tt(t2, m, kre, ALU.mult)
                    link(tt(t3, a, kim, ALU.mult))
                    tt(a, t0, t1, ALU.add)
                    link(tt(m, t2, t3, ALU.subtract))
                tt(g[:, 0, f, :], re, umb, ALU.add)
                tt(g[:, 1, f, :], um, reb, ALU.add)
                tt(g[:, 2, f, :], re, umb, ALU.subtract)
                tt(g[:, 3, f, :], um, reb, ALU.subtract).then_inc(done, 1)
                dve.wait_ge(done, f + 1)
            for n in range(8):
                par, tile = divmod(n, 4)
                dve.wait_ge(inv, n + 1)
                if order == 0:
                    tt(k.v[:, n, :], ps[:, n % 4, :], k.x1[:, n, :], ALU.mult).then_inc(fin, 1)
                else:
                    o = k.x2t[:, tile, :].rearrange("p (t r) -> p r t", r=2)[:, par, :]
                    nc.vector.scalar_tensor_tensor(o, ps[:, n % 4, :], k.inv_col[:, tile:tile + 1], o, ALU.mult, ALU.mult).then_inc(fin, 1)


def s5(k):
    nc, ps = k.nc, k.ps
    NQ, A = 4, 4
    C = 2 * A
    et, ot = ([k.at(16 * i + 8 * b, 8).rearrange("p (r d a n) -> p r d a n", r=2, d=2, a=A) for b in range(2)] for i in range(2))
    arrays = [[k.at(48 + 5 * (7 * b + i), 5).rearrange("p (c j) -> p c j", j=CH) for i in range(7)] for b in range(2)]
    uc = [k.at(118 + 5 * b, 5).rearrange("p (g j) -> p g j", j=CH) for b in range(2)]
    ll = k.at(128, 16).rearrange("p (a w n) -> p a w n", a=PAIRS, w=2)
    ys = [k.at(144 + 4 * b, 4).rearrange("p (g j) -> p g j", j=XCH) for b in range(2)]
    t3, t4 = (k.at(152 + 5 * i, 5).rearrange("p (c j) -> p c j", j=CH) for i in range(2))
    names = ("smm", "sev", "angs", "angc", "sins", "own", "pown", "omm", "oev", "llgot", "rotd", "rotp", "scan", "std", "stp")
    smm, sev, angs, angc, sins, own, pown, omm, oev, llgot, rotd, rotp, scand, std, stp = (k.sem("q_" + n) for n in names)
    ugot, tgot, ogot, yput = ([k.sem(f"q_{n}{b}") for b in range(2)] for n in ("u", "in", "out", "put"))
    with nc.Block() as block:
        @block.sync
        def _(sp):
            src = k.z_u.rearrange("(g h) s j -> s h g j", h=NH)
            lsrc = k.s5_local.rearrange("(w h) a n -> w h a n", w=2)
            dst = k.z_y.rearrange("(g h) t j -> t h g j", h=NH)

            def load(q):
                b = q % 2
                sp.dma_start(et[b].rearrange("p r d a n -> p (r d a n)"), k.s5_in[q]).then_inc(tgot[b], 16)
                for s in range(T):
                    sp.dma_start(uc[b][NH * s:NH * s + NH, :, :], src[s, :, C * q:C * q + C, :]).then_inc(ugot[b], 16)
                sp.dma_start(ot[b].rearrange("p r d a n -> p (r d a n)"), k.s5_out[q]).then_inc(ogot[b], 16)

            load(0)
            load(1)
            for w in range(2):
                for s in range(T):
                    sp.dma_start(ll[NH * s:NH * s + NH, :, w, :], lsrc[w, :, :, (T - 1 - s) * NH:(T - 1 - s) * NH + P]).then_inc(llgot, 16)
            for q in range(NQ):
                sp.wait_ge(omm, 2 * q + 2)
                if q + 2 < NQ:
                    load(q + 2)
                sp.wait_ge(oev, 2 * q + 2)
                for t in range(T):
                    sp.dma_start(dst[t, :, C * q:C * q + C, :], ys[q % 2][NH * t:NH * t + NH, :, :]).then_inc(yput[q % 2], 16)
            for b in range(2):
                sp.wait_ge(yput[b], 16 * T * 2)

        @block.tensor
        def _(pe):
            def states(q):
                b = q % 2
                pe.wait_ge(tgot[b], 16 * (q // 2 + 1))
                pe.wait_ge(ugot[b], 16 * T * (q // 2 + 1))
                for c in range(C):
                    d, a = divmod(c, A)
                    n = q * C + c
                    if n >= 4:
                        pe.wait_ge(sev, n - 3)
                    for w in range(2):
                        u = uc[b][:, 2 * a + w, :]
                        for r in range(2):
                            o = ps[NP * w:NP * w + NP, c % 4, r * CH:(r + 1) * CH]
                            lhs = et[b][:, r, d, a, NP * w:NP * w + NP]
                            if d == 0:
                                last = nc.tensor.matmul(o, lhs, u, start=True, stop=True)
                            else:
                                nc.tensor.matmul(o[:, 0:CCH], lhs, u[:, CCH - 1::-1], start=True, stop=True)
                                last = nc.tensor.matmul(o[:, CCH:CH], lhs, u[:, CH - 1:CCH - 1:-1], start=True, stop=True)
                    last.then_inc(smm, 1)

            def outputs(q):
                b = q % 2
                pe.wait_ge(ogot[b], 16 * (q // 2 + 1))
                if q == 0:
                    pe.wait_ge(llgot, 16 * 2 * T)
                pe.wait_ge(std, q + 1)
                pe.wait_ge(stp, q + 1)
                t1, t2 = arrays[b][5], arrays[b][6]
                for w in range(2):
                    if q >= 2:
                        pe.wait_ge(oev, 2 * q - 2 + w - 1)
                    for a in range(A):
                        p = slice(NP * w, NP * w + NP)
                        o = ps[:, 4 + 2 * b + w, a * P:(a + 1) * P]
                        nc.tensor.matmul(o, ll[:, A * q + a, w, :], uc[b][:, 2 * a + w, CCH:CH], start=True, stop=False)
                        for r, st in enumerate((t1, t2)):
                            nc.tensor.matmul(o, ot[b][p, r, 0, a, :], st[p, a, CCH - 1:CH - 1], start=False, stop=False)
                            last = nc.tensor.matmul(o, ot[b][p, r, 1, a, :], st[p, A + a, CH - 2:CCH - 2:-1], start=False, stop=r == 1)
                    last.then_inc(omm, 1)

            states(0)
            for q in range(NQ):
                if q + 1 < NQ:
                    states(q + 1)
                outputs(q)

        @block.scalar
        def _(act):
            def angles(q):
                cos, sin = arrays[q % 2][0:2]
                act.wait_ge(angs, q + 1)
                nc.scalar.activation(sin, sin, ACT.Sin, scale=TURN).then_inc(sins, 1)
                act.wait_ge(angc, q + 1)
                nc.scalar.activation(cos, cos, ACT.Sin, scale=TURN).then_inc(sins, 1)

            def states(q):
                bre, bim = arrays[q % 2][3:5]
                if q >= 2:
                    act.wait_ge(std, q - 1)
                    act.wait_ge(stp, q - 1)
                for c in range(C):
                    act.wait_ge(smm, q * C + c + 1)
                    nc.scalar.activation(bre[:, c, :], ps[:, c % 4, 0:CH], ACT.Copy)
                    nc.scalar.activation(bim[:, c, :], ps[:, c % 4, CH:2 * CH], ACT.Copy).then_inc(sev, 1)

            angles(0)
            states(0)
            for q in range(NQ):
                if q + 1 < NQ:
                    states(q + 1)
                    angles(q + 1)
                if q >= 2:
                    act.wait_ge(yput[q % 2], 16 * T * (q // 2))
                for w in range(2):
                    act.wait_ge(omm, 2 * q + w + 1)
                    nc.scalar.activation(ys[q % 2].rearrange("p (a w) j -> p w a j", w=2)[:, w], ps[:, 4 + 2 * (q % 2) + w, :].rearrange("p (g j) -> p g j", g=A), ACT.Copy).then_inc(oev, 1)

        flat = lambda x: x.rearrange("p c j -> p (c j)")

        @block.vector
        def _(dve):
            link = Links(dve, own)
            tt, ts = nc.vector.tensor_tensor, nc.vector.tensor_scalar

            def angles(q):
                cos, sin, dec, bre, bim, t1, t2 = arrays[q % 2]
                if q >= 2:
                    dve.wait_ge(std, q - 1)
                    dve.wait_ge(stp, q - 1)
                    dve.wait_ge(omm, 2 * q - 2)
                for d in range(2):
                    cols = slice(d * PAIRS + A * q, d * PAIRS + A * q + A)
                    link(tt(sin[:, A * d:A * d + A, :], bcast(k.tau8[:, cols], [P, A, CH]), k.steps[:, NEXP:NEXP + CH].unsqueeze(1).to_broadcast([P, A, CH]), ALU.mult))
                link(ts(t1, sin, ROUND, ROUND, ALU.add, ALU.subtract))
                link(tt(sin, sin, t1, ALU.subtract))
                ts(cos, sin, 0.25, None, ALU.add).then_inc(angs, 1)
                dve.wait_ge(angs, q + 1)
                link(ts(t1, cos, ROUND, ROUND, ALU.add, ALU.subtract))
                tt(cos, cos, t1, ALU.subtract).then_inc(angc, 1)

            angles(0)
            for q in range(NQ):
                cos, sin, dec, bre, bim, t1, t2 = arrays[q % 2]
                if q:
                    dve.wait_ge(std, q)
                dve.wait_ge(sins, 2 * q + 2)
                dve.wait_ge(sev, C * (q + 1))
                tt(t1, bre, cos, ALU.mult)
                link(tt(t3, bim, sin, ALU.mult))
                link(tt(t1, t1, t3, ALU.add))
                dve.wait_ge(rotp, q + 1)
                nc.vector.tensor_tensor_scan(flat(bre), flat(dec), flat(t1), 0.0, ALU.mult, ALU.add)
                nc.vector.tensor_tensor_scan(flat(bim), flat(dec), flat(t2), 0.0, ALU.mult, ALU.add).then_inc(scand, 1)
                dve.wait_ge(scand, q + 1)
                tt(t1, bre, cos, ALU.mult)
                link(tt(t3, bim, sin, ALU.mult))
                tt(t1, t1, t3, ALU.subtract).then_inc(std, 1)
                if q + 1 < NQ:
                    angles(q + 1)

        @block.gpsimd
        def _(pool):
            link = Links(pool, pown)
            tt, ts = nc.gpsimd.tensor_tensor, nc.gpsimd.tensor_scalar

            def factors(q):
                dec = arrays[q % 2][2]
                if q >= 2:
                    pool.wait_ge(scand, q - 1)
                for d in range(2):
                    cols = slice(d * PAIRS + A * q, d * PAIRS + A * q + A)
                    link(nc.gpsimd.tensor_copy(dec[:, A * d:A * d + A, :], bcast(k.r8[:, cols], [P, A, CH])))
                link(nc.gpsimd.memset(dec[:, :, 0:1], 0.0))

            factors(0)
            for q in range(NQ):
                cos, sin, dec, bre, bim, t1, t2 = arrays[q % 2]
                if q >= 2:
                    pool.wait_ge(omm, 2 * q - 2)
                if q:
                    pool.wait_ge(stp, q)
                pool.wait_ge(sins, 2 * q + 2)
                pool.wait_ge(sev, C * (q + 1))
                tt(t2, bim, cos, ALU.mult)
                link(tt(t4, bre, sin, ALU.mult))
                tt(t2, t2, t4, ALU.subtract).then_inc(rotp, 1)
                if q + 1 < NQ:
                    factors(q + 1)
                pool.wait_ge(scand, q + 1)
                tt(t2, bre, sin, ALU.mult)
                link(tt(t4, bim, cos, ALU.mult))
                tt(t2, t2, t4, ALU.add).then_inc(stp, 1)


def glu_and_out(k):
    nc, ps = k.nc, k.ps
    yl = k.at(0, 16).rearrange("p (q n) -> p q n", q=4)
    ul = k.at(16, 16).rearrange("p (q n) -> p q n", q=4)
    gw = k.at(48, 8).rearrange("p (q n) -> p q n", q=4)
    y5 = k.at(56, 16).rearrange("p (q n) -> p q n", q=4)
    sg = k.at(72, 8).rearrange("p (s n) -> p s n", s=4)
    wo = k.at(80, 32).rearrange("p (k n) -> p k n", k=KD)
    x2 = k.x2v
    x_high, x_low = ([k.over(f"g_x{n}{q}", at + 4 * q, 4) for q in range(4)] for n, at in (("high", 112), ("low", 32)))
    y_high, y_low = ([k.over(f"g_y{n}{q}", at + 4 * q, 4) for q in range(4)] for n, at in (("high", 16), ("low", 56)))
    w_high = [k.over(f"g_whigh{kk}", at, 4) for kk, at in enumerate((128, 132, 136, 172, 0, 4, 8, 12))]
    w_low = [k.over(f"g_wlow{kk}", 80 + 4 * kk, 4) for kk in range(KD)]
    xhi, xlo, yhi, ylo, whi, wlo = (k.sem("g_" + n) for n in ("xhi", "xlo", "yhi", "ylo", "whi", "wlo"))
    loaded, pre, gel, mm, sig, fin, got, omm, own, xg, wgot, gwgot = (k.sem("g_" + n) for n in ("load", "pre", "gelu", "mm", "sig", "fin", "got", "omm", "own", "x", "w", "gw"))
    with nc.Block() as block:
        @block.sync
        def _(sp):
            sp.dma_start(yl, k.z_y.rearrange("(q p) t j -> p q (t j)", p=P)).then_inc(loaded, 16)
            for q in range(4):
                sp.dma_start(ul[:, q, :].rearrange("p (t j) -> p t j", t=T), k.z_u[q * P:(q + 1) * P, :, CCH:CH]).then_inc(loaded, 16)
            sp.dma_start(gw, k.i["s5_glu_w"].rearrange("l (q p) n -> p (l q) n", p=P)).then_inc(gwgot, 16)
            sp.dma_start(wo, k.i["w_out"].rearrange("l (q p) n -> p (l q) n", p=P)).then_inc(wgot, 16)
            sp.dma_start(x2, k.i["x"].rearrange("b (m p) n -> p (b m) n", p=P)).then_inc(xg, 16)

        @block.vector
        def _(dve):
            link = Links(dve, own)
            for q in range(4):
                dve.wait_ge(xhi, q + 1)
                nc.vector.tensor_tensor(x_low[q], k.x2t[:, q, :], x_high[q].bitcast(F32), ALU.subtract).then_inc(xlo, 1)
            dve.wait_ge(loaded, 80)
            r = ROWS["d"][0]
            for q in range(4):
                nc.vector.scalar_tensor_tensor(yl[:, q, :], ul[:, q, :], k.cols[:, r + q:r + q + 1], yl[:, q, :], ALU.mult, ALU.add).then_inc(pre, 1)
            for n in range(8):
                q, h = divmod(n, 2)
                dve.wait_ge(sig, n + 1)
                o = y5[:, q, :].rearrange("p (j t) -> p t j", t=T)[:, 4 * h:4 * h + 4, :]
                a = yl[:, q, 512 * h:512 * h + 512].rearrange("p (t j) -> p t j", t=4)
                nc.vector.tensor_tensor(o, sg[:, n % 4, :].rearrange("p (t j) -> p t j", t=4), a, ALU.mult).then_inc(fin, 1)
            for q in range(4):
                dve.wait_ge(yhi, q + 1)
                nc.vector.tensor_tensor(y_low[q], y5[:, q, :], y_high[q].bitcast(F32), ALU.subtract).then_inc(ylo, 1)
            dve.wait_ge(xg, 16)
            for n in range(16):
                m, h = divmod(n, 2)
                dve.wait_ge(omm, n + 1)
                t = sg[:, n % 4, :]
                if n >= 4:
                    dve.wait_ge(got, n - 3)
                else:
                    dve.wait_ge(fin, 8)
                link(nc.vector.tensor_tensor(t, ps[:, 4 + n % 4, :], k.bc[:, k.G1, h * 512:(h + 1) * 512], ALU.mult))
                nc.vector.tensor_tensor(x2[:, m, h * 512:(h + 1) * 512], x2[:, m, h * 512:(h + 1) * 512], t, ALU.add).then_inc(got, 1)
                dve.wait_ge(got, n + 1)

        @block.scalar
        def _(act):
            for q in range(4):
                nc.scalar.activation(x_high[q], k.x2t[:, q, :], ACT.Copy).then_inc(xhi, 1)
            for q in range(4):
                act.wait_ge(pre, q + 1)
                nc.scalar.activation(yl[:, q, :], yl[:, q, :], ACT.Gelu_apprx_tanh).then_inc(gel, 1)
            r = ROWS["glu_b"][0]
            for n in range(8):
                q, h = divmod(n, 2)
                act.wait_ge(mm, n + 1)
                if n >= 4:
                    act.wait_ge(fin, n - 3)
                nc.scalar.activation(sg[:, n % 4, :], ps[:, n % 4, :], ACT.Sigmoid, bias=k.cols[:, r + q:r + q + 1]).then_inc(sig, 1)
                if n == 2:
                    act.wait_ge(wgot, 16)
                if 2 <= n < 6:
                    nc.scalar.activation(w_high[n - 2], wo[:, n - 2, :], ACT.Copy).then_inc(whi, 1)
            for q in range(4):
                act.wait_ge(fin, 2 * q + 2)
                nc.scalar.activation(y_high[q], y5[:, q, :], ACT.Copy).then_inc(yhi, 1)
            for kk in range(4, KD):
                nc.scalar.activation(w_high[kk], wo[:, kk, :], ACT.Copy).then_inc(whi, 1)

        @block.gpsimd
        def _(pool):
            for kk in range(KD):
                pool.wait_ge(whi, kk + 1)
                nc.gpsimd.tensor_tensor(w_low[kk], wo[:, kk, :], w_high[kk].bitcast(F32), ALU.subtract).then_inc(wlo, 1)

        @block.tensor
        def _(pe):
            pe.wait_ge(gel, 4)
            pe.wait_ge(gwgot, 16)
            for n in range(8):
                q, h = divmod(n, 2)
                if n >= 4:
                    pe.wait_ge(sig, n - 3)
                for kk in range(4):
                    last = nc.tensor.matmul(ps[:, n % 4, :], gw[:, kk, q * P:(q + 1) * P], yl[:, kk, 512 * h:512 * h + 512], start=kk == 0, stop=kk == 3)
                last.then_inc(mm, 1)

            def products(n, tiles):
                m, h = divmod(n, 2)
                t, f = slice(m * P, (m + 1) * P), slice(h * 512, (h + 1) * 512)
                for kk in tiles:
                    xh, xl = ((x_high, x_low) if kk < 4 else (y_high, y_low))
                    o = ps[:, 4 + n % 4, :]
                    nc.tensor.matmul(o, xh[kk % 4][:, t], w_high[kk][:, f], start=kk == 0, stop=False)
                    nc.tensor.matmul(o, xh[kk % 4][:, t], w_low[kk][:, f], start=False, stop=False)
                    last = nc.tensor.matmul(o, xl[kk % 4][:, t], w_high[kk][:, f], start=False, stop=kk == KD - 1)
                return last

            pe.wait_ge(xlo, 4)
            pe.wait_ge(wlo, 4)
            for n in range(4):
                products(n, range(4))
            pe.wait_ge(ylo, 4)
            pe.wait_ge(wlo, 8)
            for n in range(16):
                if n >= 4:
                    pe.wait_ge(got, n - 3)
                products(n, range(4 if n < 4 else 0, KD)).then_inc(omm, 1)


def route(k):
    nc, ps = k.nc, k.ps
    x2 = k.x2v
    h2 = k.at(96, 12).rearrange("p (s n) -> p s n", s=3)
    h2t = k.at(108, 8).rearrange("p (s n) -> p s n", s=2)
    sq = k.at(116, 4)
    rw = k.at(120, 1)[:, 0:128].rearrange("p (k e) -> p k e", k=KD)
    lg = k.at(121, 1)[:, 0:128].rearrange("p (m e) -> p m e", m=8)
    red = k.at(122, 1)[:, 0:32]
    aff = k.at(124, 4)[0:NE, :]
    vals = k.at(128, 1)[0:NE, 0:CAP]
    idx = k.at(129, 1)[0:NE, 0:CAP].bitcast(U32)
    idf = k.at(130, 1)[0:NE, 0:CAP]
    loaded, ss, mean, rt, hh, own, tr, tev, lmm, ex, atr, own3, ftr, exd = (k.sem("r_" + n) for n in ("load", "ss", "mean", "sqrt", "h2", "own", "tr", "tev", "lmm", "exp", "atr", "own3", "ftr", "exd"))
    put = [k.sem(f"r_put{s}") for s in range(3)]
    spilled = k.sem("r_spilled")
    with nc.Block() as block:
        @block.sync
        def _(sp):
            sp.dma_start(rw, k.i["router_w"].rearrange("l (k p) e -> p (l k) e", p=P)).then_inc(loaded, 16)
            for m in range(8):
                sp.wait_ge(hh, m + 1)
                sp.dma_start(k.h2[m * P:(m + 1) * P, :], h2[:, m % 3, :]).then_inc(put[m % 3], 16)
            sp.dma_start(k.x2d.rearrange("(m p) n -> p m n", p=P), x2).then_inc(spilled, 16)
            for n in range(k.weights.NS):
                k.weights.load(sp, 0, n)
            for s in range(3):
                sp.wait_ge(put[s], 16 * len(range(s, 8, 3)))
            sp.wait_ge(spilled, 16)

        @block.scalar
        def _(act):
            for m in range(8):
                if m:
                    act.wait_ge(ss, m)
                nc.scalar.activation(sq, x2[:, m, :], ACT.Square, accum_out=k.rstd[:, m:m + 1]).then_inc(ss, 1)
            act.wait_ge(mean, 1)
            nc.scalar.activation(k.rstd[:, 0:8], k.rstd[:, 0:8], ACT.Sqrt).then_inc(rt, 1)
            for m in range(8):
                act.wait_ge(tr, m + 1)
                if m >= 2:
                    act.wait_ge(lmm, m - 1)
                nc.scalar.activation(h2t[:, m % 2, :], ps[:, 2 * (m % 2):2 * (m % 2) + 2, :].rearrange("p b n -> p (b n)"), ACT.Copy).then_inc(tev, 1)
            act.wait_ge(ex, 1)
            nc.scalar.activation(lg, lg, ACT.Exp).then_inc(exd, 1)

        def logits(pe, m):
            pe.wait_ge(tev, m + 1)
            for kk in range(KD):
                last = nc.tensor.matmul(ps[:, 4, m * NE:(m + 1) * NE], h2t[:, m % 2, kk * P:(kk + 1) * P], rw[:, kk, :], start=kk == 0, stop=kk == KD - 1)
            last.then_inc(lmm, 1)

        @block.tensor
        def _(pe):
            pe.wait_ge(loaded, 16)
            for m in range(8):
                pe.wait_ge(hh, m + 1)
                if m >= 2:
                    pe.wait_ge(tev, m - 1)
                for kk in range(KD):
                    last = nc.tensor.transpose(ps[:, 2 * (m % 2) + kk // 4, (kk % 4) * P:(kk % 4 + 1) * P], h2[:, m % 3, kk * P:(kk + 1) * P], k.ident)
                last.then_inc(tr, 1)
                if m:
                    logits(pe, m - 1)
            logits(pe, 7)
            pe.wait_ge(ex, 2)
            for m in range(8):
                last = nc.tensor.transpose(ps[0:NE, 5 + m // 4, (m % 4) * P:(m % 4 + 1) * P], lg[:, m, :], k.ident)
            last.then_inc(atr, 1)
            pe.wait_ge(ex, 3)
            nc.tensor.transpose(ps[:, 4, 0:NE], vals, k.ident[0:NE, 0:NE])
            nc.tensor.transpose(ps[:, 4, NE:2 * NE], idf, k.ident[0:NE, 0:NE]).then_inc(ftr, 1)

        @block.vector
        def _(dve):
            link = Links(dve, own)
            dve.wait_ge(ss, 8)
            r = k.rstd[:, 0:8]
            nc.vector.tensor_scalar(r, r, 1.0 / D, EPS, ALU.mult, ALU.add).then_inc(mean, 1)
            dve.wait_ge(rt, 1)
            link(nc.vector.reciprocal(r, r))
            for m in range(8):
                if m >= 3:
                    dve.wait_ge(put[m % 3], 16 * (m // 3))
                    dve.wait_ge(tr, m - 2)
                o = h2[:, m % 3, :]
                link(nc.vector.scalar_tensor_tensor(o, x2[:, m, :], k.rstd[:, m:m + 1], k.bc[:, k.A2, :], ALU.mult, ALU.mult))
                nc.vector.tensor_tensor(o, o, k.bc[:, k.SH2, :], ALU.add).then_inc(hh, 1)
            dve.wait_ge(lmm, 8)
            z = ps[:, 4, 0:128].rearrange("p (m e) -> p m e", m=8)
            mx, sm = red[:, 0:8], red[:, 8:16]
            link(nc.vector.tensor_reduce(mx, z, AX.X, ALU.max))
            nc.vector.tensor_tensor(lg, z, bcast(mx, [P, 8, NE]), ALU.subtract).then_inc(ex, 1)
            dve.wait_ge(exd, 1)
            link(nc.vector.tensor_reduce(sm, lg, AX.X, ALU.add))
            link(nc.vector.reciprocal(sm, sm))
            nc.vector.tensor_tensor(lg, lg, bcast(sm, [P, 8, NE]), ALU.mult).then_inc(ex, 1)
            dve.wait_ge(atr, 1)
            link(nc.vector.tensor_copy(aff, ps[0:NE, 5:7, :].rearrange("p b n -> p (b n)")))
            for i in range(CAP // 8):
                s = slice(8 * i, 8 * i + 8)
                link(nc.vector.max(vals[:, s], aff))
                nc.vector.max_index(idx[:, s], vals[:, s], aff)
                link(nc.vector.match_replace(aff, vals[:, s], aff, -1.0))
            nc.vector.tensor_copy(idf, idx).then_inc(ex, 1)
            dve.wait_ge(ftr, 1)
            nc.vector.tensor_copy(k.gate_t, ps[:, 4, 0:NE])
            link(nc.vector.tensor_copy(k.idx_t, ps[:, 4, NE:2 * NE]))


class Weights:

    W = 512
    widths = [(f, min(512, FF - f)) for f in range(0, FF, 512)]
    NCW = len(widths)
    FT = FF // P
    NS, NHI = 6, 3
    UNITS = 3 * NCW
    DOWN = 2 * NCW
    tiles = [min(4, FF // P - 4 * c) for c in range(NCW)]

    def __init__(self, k):
        assert self.UNITS % self.NS == 0 and self.UNITS % self.NHI == 0
        self.raw = [k.over(f"w_raw{s}", 16 * s, 16, F32) for s in range(self.NS)]
        self.got = [k.ctx.enter_context(k.nc.semaphore(f"e_got{s}")) for s in range(self.NS)]
        self.gate_up = [k.i[n].rearrange("l e (k p) f -> l e p k f", p=P) for n in ("ex_w_gate", "ex_w_up")]
        self.down = k.i["ex_w_down"].rearrange("l e (f p) n -> l e p f n", p=P)

    def elements(self, n):
        return KD * self.widths[n // 2][1] if n < self.DOWN else self.tiles[n - self.DOWN] * D

    def load(self, eng, e, n):
        s, w = n % self.NS, self.elements(n)
        if n < self.DOWN:
            f0, cols = self.widths[n // 2]
            src = self.gate_up[n % 2][0, bass.ds(e, 1), :, :, f0:f0 + cols].rearrange("e p k f -> p (e k) f")
            dst = self.raw[s][:, 0:w].rearrange("p (k f) -> p k f", k=KD)
        else:
            c = n - self.DOWN
            src = self.down[0, bass.ds(e, 1), :, 4 * c:4 * c + self.tiles[c], :].rearrange("e p f n -> p (e f) n")
            dst = self.raw[s][:, 0:w].rearrange("p (f n) -> p f n", f=self.tiles[c])
        eng.dma_start(dst, src).then_inc(self.got[s], 16)


def experts(k):
    nc, ps = k.nc, k.ps
    wt = k.weights
    widths, NCW, FT, NS, NHI, UNITS, DOWN, tiles = wt.widths, wt.NCW, wt.FT, wt.NS, wt.NHI, wt.UNITS, wt.DOWN, wt.tiles
    raw, got, elements = wt.raw, wt.got, wt.elements
    XT_AT = DOWN + 3
    low = [k.over(f"w_low{s}", 16 * s, 16) for s in range(NS)]
    high = [k.over(f"w_high{s}", 16 * (NS + s), 16) for s in range(NHI)]
    xe = k.at(144, 4)
    xt_h, xt_l = k.over("x_high", 148, 4), k.over("x_low", 152, 4)
    at_h, at_l = k.over("a_high", 156, 11), k.over("a_low", 167, 11)
    xt_f, at_f = xt_h.bitcast(F32), at_h.bitcast(F32)
    act_ = k.at(178, 4).rearrange("p (s n) -> p s n", s=2)
    sg = k.at(182, 4).rearrange("p (s n) -> p s n", s=2)
    ye = k.extra
    idx_next = k.small[:, 453:454].bitcast(U32)
    spare = k.small[0:1, 480:481]
    zero = k.small[:, 481:482].bitcast(I32)
    used, hi_done, lo_done, idxr, gat, xtr, xev, silu, amul, atr, ahi, alo, yev, put, spared = (
        k.sem("e_" + n) for n in ("used", "high", "low", "idx", "gather", "xtr", "xev", "silu", "amul", "atr", "ahi", "alo", "yev", "put", "spared"))
    xhi = k.sem("e_xhi")

    def experts_of(eng, body):
        with eng.Fori(0, NE - 1) as e:
            body(e, False)
        body(NE - 1, True)

    def multiplied(e, n):
        return e * UNITS + n + 1 + NS

    def which(e):
        return bass.ds(e, 1)

    with nc.Block() as block:
        @block.sync
        def _(sp):
            def loads(e, first):
                for n in range(first, UNITS):
                    sp.wait_ge(used, multiplied(e, n - NS))
                    wt.load(sp, e, n)
            loads(0, NS)
            with sp.Fori(1, NE) as e:
                loads(e, 0)

        @block.gpsimd
        def _(pool):
            nc.gpsimd.memset(spare, 0.0).then_inc(spared, 1)
            nc.gpsimd.memset(zero, 0).then_inc(spared, 1)
            pool.wait_ge(spared, 2)
            nc.gpsimd.tensor_tensor(k.idx_now.bitcast(I32), k.idx_t[:, 0:1], zero, ALU.add).then_inc(idxr, 1)
            pool.wait_ge(idxr, 1)
            pool.indirect_dma_start(xe, None, k.h2, bass.IndirectOffsetOnAxis(ap=k.idx_now, axis=0)).then_inc(gat, 16)

            def tokens(e, last):
                if not last:
                    nc.gpsimd.tensor_tensor(idx_next.bitcast(I32), k.idx_t[:, bass.ds(e + 1, 1)], zero, ALU.add).then_inc(idxr, 1)
                    pool.wait_ge(idxr, 2 * e + 2)
                    pool.wait_ge(xtr, e + 1)
                    pool.wait_ge(spared, 2 * e + 2)
                    nc.gpsimd.tensor_tensor(spare, spare, spare, ALU.add).then_inc(spared, 1)
                    pool.indirect_dma_start(xe, None, k.h2, bass.IndirectOffsetOnAxis(ap=idx_next, axis=0)).then_inc(gat, 16)
                    pool.wait_ge(gat, e * 16 + 32)
                pool.wait_ge(yev, e + 2)
                if not last:
                    pool.wait_ge(spared, 2 * e + 3)
                    nc.gpsimd.tensor_tensor(spare, spare, spare, ALU.add).then_inc(spared, 1)
                pool.indirect_dma_start(k.moe, bass.IndirectOffsetOnAxis(ap=k.idx_now, axis=0), ye, None, compute_op=ALU.add).then_inc(put, 16)
                pool.wait_ge(put, e * 16 + 16)
                if not last:
                    nc.gpsimd.tensor_tensor(k.idx_now.bitcast(I32), idx_next.bitcast(I32), zero, ALU.add).then_inc(idxr, 1)
                    pool.wait_ge(idxr, 2 * e + 3)
            experts_of(pool, tokens)

        @block.tensor
        def _(pe):
            def transpose_tokens(gathered):
                pe.wait_ge(gat, gathered)
                for kk in range(KD):
                    last = nc.tensor.transpose(ps[:, 4 + kk // 4, (kk % 4) * P:(kk % 4 + 1) * P], xe[:, kk * P:(kk + 1) * P], k.ident)
                last.then_inc(xtr, 1)

            def transpose_act(e, c):
                pe.wait_ge(amul, e * NCW + c + 1)
                for i in range(tiles[c]):
                    last = nc.tensor.transpose(ps[:, 4 + c % 2, i * P:(i + 1) * P], act_[:, c % 2, i * P:(i + 1) * P], k.ident)
                last.then_inc(atr, 1)

            def products(e, last_e):
                pe.wait_ge(xev, e + 1)
                for n in range(UNITS):
                    pe.wait_ge(lo_done, e * UNITS + n + 1)
                    h, l = high[n % NHI], low[n % NS]
                    if n < DOWN:
                        c, w = n // 2, widths[n // 2][1]
                        if c >= 2 and n % 2 == 0:
                            pe.wait_ge(amul, e * NCW + c - 1)
                        for kk in range(KD):
                            x = slice(kk * P, (kk + 1) * P)
                            f = slice(kk * w, (kk + 1) * w)
                            o = ps[:, 2 * (c % 2) + n % 2, 0:w]
                            nc.tensor.matmul(o, xt_h[:, x], h[:, f], start=kk == 0, stop=False)
                            nc.tensor.matmul(o, xt_h[:, x], l[:, f], start=False, stop=False)
                            last = nc.tensor.matmul(o, xt_l[:, x], h[:, f], start=False, stop=kk == KD - 1)
                    else:
                        c = n - DOWN
                        pe.wait_ge(alo, e * NCW + c + 1)
                        if c == 0:
                            pe.wait_ge(yev, e + 1)
                        for i in range(tiles[c]):
                            f = 4 * c + i
                            a = slice(f * P, (f + 1) * P)
                            for x, m, first in ((at_h, h, True), (at_h, l, False), (at_l, h, False)):
                                for half in range(2):
                                    last = nc.tensor.matmul(ps[:, 6 + half, :], x[:, a], m[:, i * D + half * 512:i * D + (half + 1) * 512],
                                                            start=f == 0 and first, stop=f == FT - 1 and x is at_l)
                    last.then_inc(used, 1)
                    if n % 2 == 0 and 2 <= n <= DOWN:
                        transpose_act(e, n // 2 - 1)
                    if n == XT_AT and not last_e:
                        transpose_tokens(e * 16 + 32)

            pe.sem_inc(used, NS)
            transpose_tokens(16)
            experts_of(pe, products)

        @block.scalar
        def _(act):
            def high_part(e, n):
                act.wait_ge(got[n % NS], e * (16 * UNITS // NS) + 16 * (n // NS + 1))
                act.wait_ge(used, multiplied(e, n - NHI))
                w = elements(n)
                nc.scalar.activation(high[n % NHI][:, 0:w], raw[n % NS][:, 0:w], ACT.Copy).then_inc(hi_done, 1)

            def high_tokens(e):
                act.wait_ge(xtr, e + 1)
                nc.scalar.activation(xt_h, ps[:, 4:6, :].rearrange("p b n -> p (b n)"), ACT.Copy).then_inc(xhi, 1)

            def step(e, last_e):
                for n in range(UNITS):
                    if n % 2 == 0 and 2 <= n <= DOWN:
                        c = n // 2 - 1
                        w = widths[c][1]
                        act.wait_ge(used, multiplied(e, n - 1))
                        nc.scalar.activation(sg[:, c % 2, 0:w], ps[:, 2 * (c % 2), 0:w], ACT.Silu).then_inc(silu, 1)
                    if n % 2 == 1 and 3 <= n <= DOWN + 1:
                        c = (n - 3) // 2
                        act.wait_ge(atr, e * NCW + c + 1)
                        nc.scalar.activation(at_h[:, 4 * c * P:(4 * c + tiles[c]) * P], ps[:, 4 + c % 2, 0:tiles[c] * P], ACT.Copy).then_inc(ahi, 1)
                    if n == XT_AT + 1 and not last_e:
                        high_tokens(e + 1)
                    if n + 2 < UNITS:
                        high_part(e, n + 2)
                    elif not last_e:
                        high_part(e + 1, n + 2 - UNITS)

            high_tokens(0)
            high_part(0, 0)
            high_part(0, 1)
            experts_of(act, step)

        @block.vector
        def _(dve):
            def low_part(e, n):
                dve.wait_ge(hi_done, e * UNITS + n + 1)
                w = elements(n)
                nc.vector.tensor_tensor(low[n % NS][:, 0:w], raw[n % NS][:, 0:w], high[n % NHI][:, 0:w].bitcast(F32), ALU.subtract).then_inc(lo_done, 1)

            def low_tokens(e):
                dve.wait_ge(xhi, e + 1)
                nc.vector.tensor_tensor(xt_l, ps[:, 4:6, :].rearrange("p b n -> p (b n)"), xt_f, ALU.subtract).then_inc(xev, 1)

            def step(e, last_e):
                for n in range(UNITS):
                    if n % 2 == 0 and 2 <= n <= DOWN:
                        c = n // 2 - 1
                        w = widths[c][1]
                        dve.wait_ge(silu, e * NCW + c + 1)
                        nc.vector.tensor_tensor(act_[:, c % 2, 0:w], sg[:, c % 2, 0:w], ps[:, 2 * (c % 2) + 1, 0:w], ALU.mult).then_inc(amul, 1)
                    if n % 2 == 1 and 3 <= n <= DOWN + 1:
                        c = (n - 3) // 2
                        a = slice(4 * c * P, (4 * c + tiles[c]) * P)
                        dve.wait_ge(ahi, e * NCW + c + 1)
                        nc.vector.tensor_tensor(at_l[:, a], ps[:, 4 + c % 2, 0:tiles[c] * P], at_f[:, a], ALU.subtract).then_inc(alo, 1)
                    if n == XT_AT + 1 and not last_e:
                        low_tokens(e + 1)
                    if n + 1 < UNITS:
                        low_part(e, n + 1)
                    elif not last_e:
                        low_part(e + 1, 0)
                dve.wait_ge(used, multiplied(e, UNITS - 1))
                dve.wait_ge(idxr, 2 * e + 1)
                nc.vector.tensor_scalar(ye, ps[:, 6:8, :].rearrange("p b n -> p (b n)"), k.gate_t[:, which(e)], None, ALU.mult).then_inc(yev, 1)

            dve.sem_inc(yev, 1)
            low_tokens(0)
            low_part(0, 0)
            experts_of(dve, step)


def finish(k):
    nc = k.nc
    x2 = k.x2v
    m_ = k.at(0, 32).rearrange("p (m n) -> p m n", m=8)
    sq = k.at(32, 4)
    add, ss, mean, rt, put, own = (k.sem("z_" + n) for n in ("add", "ss", "mean", "sqrt", "put", "own"))
    outd, got = k.sem("z_out"), [k.sem(f"z_load{m}") for m in range(8)]
    with nc.Block() as block:
        @block.sync
        def _(sp):
            for m in range(8):
                sp.dma_start(x2[:, m, :], k.x2d[m * P:(m + 1) * P, :]).then_inc(got[m], 16)
                sp.dma_start(m_[:, m, :], k.moe[m * P:(m + 1) * P, :]).then_inc(got[m], 16)
            for m in range(8):
                sp.wait_ge(put, m + 1)
                sp.dma_start(k.out[0, m * P:(m + 1) * P, :], m_[:, m, :]).then_inc(outd, 16)
            sp.wait_ge(outd, 128)

        @block.scalar
        def _(act):
            for m in range(8):
                act.wait_ge(add, m + 1)
                if m:
                    act.wait_ge(rt, m)
                nc.scalar.activation(sq, x2[:, m, :], ACT.Square, accum_out=k.rstd[:, m:m + 1]).then_inc(ss, 1)
                act.wait_ge(mean, m + 1)
                nc.scalar.activation(k.rstd[:, m:m + 1], k.rstd[:, m:m + 1], ACT.Sqrt).then_inc(rt, 1)

        @block.vector
        def _(dve):
            link = Links(dve, own)

            def scaled(m):
                r = k.rstd[:, m:m + 1]
                dve.wait_ge(rt, m + 1)
                link(nc.vector.reciprocal(r, r))
                nc.vector.scalar_tensor_tensor(m_[:, m, :], x2[:, m, :], r, k.bc[:, k.FG, :], ALU.mult, ALU.mult).then_inc(put, 1)

            for m in range(8):
                dve.wait_ge(got[m], 32)
                link(nc.vector.tensor_tensor(m_[:, m, :], m_[:, m, :], k.bc[:, k.G2, :], ALU.mult))
                nc.vector.tensor_tensor(x2[:, m, :], x2[:, m, :], m_[:, m, :], ALU.add).then_inc(add, 1)
                if m:
                    scaled(m - 1)
                dve.wait_ge(ss, m + 1)
                dve.wait_ge(add, m + 1)
                r = k.rstd[:, m:m + 1]
                nc.vector.tensor_scalar(r, r, 1.0 / D, EPS, ALU.mult, ALU.add).then_inc(mean, 1)
            scaled(7)


def build(nc, ins, consts, out, until=99):
    with ExitStack() as ctx:
        k = Core(nc, ctx, ins, consts, out)
        k.x2v = k.at(140, 32).rearrange("p (m n) -> p m n", m=8)
        k.weights = Weights(k)
        stages = [lambda: modulation(k), lambda: filters(k, 0), lambda: projection(k), lambda: long_conv(k, 0), lambda: filters(k, 1),
                  lambda: long_conv(k, 1), lambda: s5(k), lambda: glu_and_out(k), lambda: route(k), lambda: experts(k), lambda: finish(k)]
        for s in stages[:until]:
            s()
            k.end_stage()


_INS = ["x", "c", "ctx", "c_ctx", "mod_w", "mod_b", "norm1_g", "norm2_g", "w_in", "w_out", "conv_w", "conv_b",
        "hy_w1", "hy_b1", "hy_freq", "hy_w2", "hy_b2", "hy_w3", "hy_b3", "hy_bias",
        "s5_lam_re", "s5_lam_im", "s5_log_step", "s5_b_re", "s5_b_im", "s5_c_re", "s5_c_im", "s5_d",
        "s5_glu_w", "s5_glu_b", "router_w", "ex_w_gate", "ex_w_up", "ex_w_down", "final_g"]


def kernel(**inputs):
    import numpy as _np
    import concourse.bacc as _bacc
    from concourse import mybir as _mybir
    from concourse.bass_utils import run_bass_kernel_spmd as _run

    nc = _bacc.Bacc("TRN2", target_bir_lowering=False, num_devices=1)
    arrays, ins, consts = {}, {}, {}
    for name in _INS:
        a = _np.ascontiguousarray(inputs[name])
        arrays[f"in_{name}"] = a
        ins[name] = nc.dram_tensor(f"in_{name}", a.shape, _mybir.dt.from_np(a.dtype), kind="ExternalInput").ap()
    for name, a in shape_constants().items():
        arrays[f"const_{name}"] = a
        consts[name] = nc.dram_tensor(f"const_{name}", a.shape, _mybir.dt.from_np(a.dtype), kind="ExternalInput").ap()
    out = nc.dram_tensor("out", (1, SEQ, D), _mybir.dt.float32, kind="ExternalOutput").ap()
    build(nc, ins, consts, out)
    r = _run(nc, [arrays], core_ids=[0])
    return r.results[0]["out"]
```
